# Optimizing a Trainium2 kernel written in Bass

```python
import math
import jax, jax.numpy as jnp
from jax import lax
import numpy as np

D_MODEL = 1024
BATCH = 1
SEQ = 256
DEPTH = 1

GRID_W = 64
CTX_LEN = 256
N_BRANCH = 3
D_BR = D_MODEL // 2
HY_ORDER = 2
HY_BANDS = 16
HY_POS_DIM = 1 + 2 * HY_BANDS
HY_FILTER_HID = 64
HY_DECAY_SLOW = 3.07
HY_DECAY_FAST = 15.35
FN_GROUPS = 4
FN_GROUP_W = D_BR // FN_GROUPS
ML_HEADS = 4
ML_HD = D_BR // ML_HEADS
ML_CHUNK = 128
ML_FGATE_LO = 3.0
ML_FGATE_HI = 6.0
P_HY = 3 * D_BR
P_FN = D_BR
P_ML = 4 * D_BR
P_MLG = 4 * ML_HEADS
P_GATE = N_BRANCH * D_MODEL
OFF_FN = P_HY
OFF_ML = OFF_FN + P_FN
OFF_MLG = OFF_ML + P_ML
OFF_GATE = OFF_MLG + P_MLG
P_TOT = OFF_GATE + P_GATE
MOE_GROUPS = 4
MOE_PER_GROUP = 4
MOE_EXPERTS = MOE_GROUPS * MOE_PER_GROUP
MOE_TOPK = 2
EXPERT_HID = D_MODEL // 4
EPS = 1e-6


def rmsnorm(x, w):
    xf = x.astype(jnp.float32)
    y = xf * lax.rsqrt(jnp.mean(xf * xf, axis=-1, keepdims=True) + EPS)
    return (y * w.astype(jnp.float32)).astype(x.dtype)

def modulate(h, shift, scale):
    return h * (1 + scale) + shift

def dwconv_grid(u, w, b, grid):
    B, L, C = u.shape
    rows, width = grid
    img = u.reshape(B, rows, width, C)
    out = lax.conv_general_dilated(img, w[:, :, None, :].astype(u.dtype), (1, 1), "SAME",
                                   dimension_numbers=("NHWC", "HWIO", "NHWC"),
                                   feature_group_count=C)
    return out.reshape(B, L, C) + b.astype(u.dtype)

def hyena_filter(L, lp):
    f32 = jnp.float32
    t = jnp.arange(L, dtype=f32) / L
    bands = jnp.linspace(1e-4, HY_BANDS - 1, HY_BANDS, dtype=f32)
    ang = (2 * math.pi) * t[:, None] * bands[None, :]
    feats = jnp.concatenate([t[:, None], jnp.cos(ang), jnp.sin(ang)], axis=-1)
    freq = lp["hy_f_freq"].astype(f32)
    h = jnp.sin(freq * (feats @ lp["hy_f_w1"].astype(f32) + lp["hy_f_b1"].astype(f32)))
    h = jnp.sin(freq * (h @ lp["hy_f_w2"].astype(f32) + lp["hy_f_b2"].astype(f32)))
    h = (h @ lp["hy_f_w3"].astype(f32)).reshape(L, HY_ORDER, 2, D_BR)
    h = h * jnp.exp(-t[:, None, None, None] * jnp.abs(lp["hy_decay"].astype(f32)))
    fwd, bwd = h[:, :, 0], h[:, :, 1]
    k = jnp.concatenate([fwd, jnp.zeros_like(fwd[:1]), jnp.flip(bwd[1:], axis=0)], axis=0)
    k = k * lax.rsqrt(jnp.sum(k * k, axis=0, keepdims=True) + EPS)
    return jnp.fft.rfft(k, axis=0)

def fft_longconv(u, kf, skip):
    L = u.shape[1]
    uf = jnp.fft.rfft(u, n=2 * L, axis=1)
    y = jnp.fft.irfft(uf * kf[None], n=2 * L, axis=1)[:, :L]
    return y + u * skip

def hyena_branch(zh, grid, lp):
    L = zh.shape[1]
    u = dwconv_grid(zh, lp["hy_conv_w"], lp["hy_conv_b"], grid).astype(jnp.float32)
    v, x1, x2 = jnp.split(u, 3, axis=-1)
    kf = hyena_filter(L, lp)
    skip = lp["hy_skip"].astype(jnp.float32)
    z = x1 * fft_longconv(v, kf[:, 0], skip[0])
    return x2 * fft_longconv(z, kf[:, 1], skip[1])

def fnet_branch(zf):
    B, L, _ = zf.shape
    u = zf.astype(jnp.float32).reshape(B, L, FN_GROUPS, FN_GROUP_W)
    y = jnp.fft.fft2(u, axes=(1, 3), norm="ortho").real
    return y.reshape(B, L, D_BR)

def zero_state(batch):
    f32 = jnp.float32
    return (jnp.zeros((batch, ML_HEADS, ML_HD, ML_HD), f32),
            jnp.zeros((batch, ML_HEADS, ML_HD), f32),
            jnp.zeros((batch, ML_HEADS), f32))

def mlstm_scan(q, k, v, i_pre, f_pre, state):
    B, H, L, d = q.shape
    T = ML_CHUNK
    nc = L // T

    def chunks(a):
        return jnp.moveaxis(a.reshape((B, H, nc, T) + a.shape[3:]), 2, 0)

    q = q * (d ** -0.5)
    logf = jax.nn.log_sigmoid(f_pre)
    mask = jnp.tril(jnp.ones((T, T), dtype=bool))

    def step(carry, inp):
        C, n, m = carry
        qc, kc, vc, ic, lfc = inp
        b = jnp.cumsum(lfc, axis=-1)
        Dm = jnp.where(mask, b[..., :, None] - b[..., None, :] + ic[..., None, :], -jnp.inf)
        inter = b + m[..., None]
        m_row = jnp.maximum(inter, jnp.max(Dm, axis=-1))
        w_intra = jnp.exp(Dm - m_row[..., None])
        w_inter = jnp.exp(inter - m_row)
        s = jnp.einsum("bhtk,bhsk->bhts", qc, kc) * w_intra
        num = jnp.einsum("bhts,bhsv->bhtv", s, vc) + w_inter[..., None] * jnp.einsum("bhvk,bhtk->bhtv", C, qc)
        den = jnp.sum(s, axis=-1) + w_inter * jnp.einsum("bhk,bhtk->bht", n, qc)
        den = jnp.maximum(jnp.abs(den), jnp.exp(-m_row))
        h = num / den[..., None]
        bT = b[..., -1]
        a = bT[..., None] - b + ic
        m_new = jnp.maximum(bT + m, jnp.max(a, axis=-1))
        sc = jnp.exp(a - m_new[..., None])
        decay = jnp.exp(bT + m - m_new)
        C_new = decay[..., None, None] * C + jnp.einsum("bhs,bhsv,bhsk->bhvk", sc, vc, kc)
        n_new = decay[..., None] * n + jnp.einsum("bhs,bhsk->bhk", sc, kc)
        return (C_new, n_new, m_new), h

    state, h = lax.scan(step, state, (chunks(q), chunks(k), chunks(v), chunks(i_pre), chunks(logf)))
    return jnp.moveaxis(h, 0, 2).reshape(B, H, L, d), state

def mlstm_branch(zm, zg, grid, lp, state_f, state_b):
    B, L, _ = zm.shape
    qk = jax.nn.silu(dwconv_grid(zm[..., :2 * D_BR], lp["ml_conv_w"], lp["ml_conv_b"], grid))
    v = zm[..., 2 * D_BR:3 * D_BR]
    o = zm[..., 3 * D_BR:]

    def heads(a):
        return a.reshape(B, L, ML_HEADS, ML_HD).transpose(0, 2, 1, 3).astype(jnp.float32)

    q, k, v = heads(qk[..., :D_BR]), heads(qk[..., D_BR:]), heads(v)
    g = zg.astype(jnp.float32).reshape(B, L, 4, ML_HEADS).transpose(2, 0, 3, 1)
    h_f, st_f = mlstm_scan(q, k, v, g[0], g[1], state_f)
    rev = lambda a: jnp.flip(a, axis=2)
    h_b, st_b = mlstm_scan(rev(q), rev(k), rev(v), rev(g[2]), rev(g[3]), state_b)
    h = h_f + rev(h_b)
    h = h * lax.rsqrt(jnp.mean(h * h, axis=-1, keepdims=True) + EPS)
    h = h.transpose(0, 2, 1, 3).reshape(B, L, D_BR) * lp["ml_norm_w"].astype(jnp.float32)
    return jax.nn.sigmoid(o.astype(jnp.float32)) * h, st_f, st_b

def merge_branches(y_hy, y_fn, y_ml, gate_pre, lp):
    B, L, _ = gate_pre.shape
    dt = gate_pre.dtype
    ys = jnp.stack([y_hy, y_fn, y_ml], axis=2).astype(dt)
    proj = jnp.einsum("blkc,kcd->blkd", ys, lp["w_branch"])
    g = jax.nn.sigmoid(gate_pre.astype(jnp.float32)).reshape(B, L, N_BRANCH, D_MODEL).astype(dt)
    return jnp.sum(g * proj, axis=2) @ lp["w_out"]

def token_mixer_out(z, grid, lp, ml_out):
    y_hy = hyena_branch(z[..., :OFF_FN], grid, lp)
    y_fn = fnet_branch(z[..., OFF_FN:OFF_ML])
    return merge_branches(y_hy, y_fn, ml_out, z[..., OFF_GATE:], lp)

def hier_moe(h, lp):
    B, L, D = h.shape
    t = h.reshape(B * L, D)
    g_logits = (t @ lp["moe_rg_w"] + lp["moe_rg_b"]).astype(jnp.float32)
    p_top, g_sel = lax.top_k(jax.nn.softmax(g_logits, axis=-1), 1)
    e_logits = (t @ lp["moe_re_w"] + lp["moe_re_b"]).astype(jnp.float32).reshape(B * L, MOE_GROUPS, MOE_PER_GROUP)
    g_onehot = jax.nn.one_hot(g_sel[:, 0], MOE_GROUPS, dtype=jnp.float32)
    e_in_group = jnp.sum(e_logits * g_onehot[:, :, None], axis=1)
    e_top, e_sel = lax.top_k(e_in_group, MOE_TOPK)
    w_sel = p_top * jax.nn.softmax(e_top, axis=-1)
    e_idx = g_sel * MOE_PER_GROUP + e_sel
    combine = jnp.sum(jax.nn.one_hot(e_idx, MOE_EXPERTS, dtype=jnp.float32) * w_sel[..., None], axis=1)
    hg = jnp.einsum("nd,edh->neh", t, lp["moe_w_gate"])
    hu = jnp.einsum("nd,edh->neh", t, lp["moe_w_up"])
    a = jax.nn.silu(hg) * hu * combine[..., None].astype(t.dtype)
    return jnp.einsum("neh,ehd->nd", a, lp["moe_w_down"]).reshape(B, L, D)

def first_inputs(seed: int = 0) -> dict:
    key = jax.random.key(seed)
    ks = iter(jax.random.split(key, 40))
    f32 = jnp.float32

    def nrm(shape, scale):
        return jax.random.normal(next(ks), shape, f32) * scale

    x = nrm((BATCH, SEQ, D_MODEL), 1.0)
    c = nrm((BATCH, D_MODEL), 1.0)
    ctx = nrm((BATCH, CTX_LEN, D_MODEL), 1.0)
    c_ctx = nrm((D_MODEL,), 1.0)
    ada_w = nrm((DEPTH, D_MODEL, 6 * D_MODEL), 0.5 * D_MODEL ** -0.5)
    ada_b = nrm((DEPTH, 6 * D_MODEL), 0.02)
    norm1_w = 1.0 + nrm((DEPTH, D_MODEL), 0.02)
    norm2_w = 1.0 + nrm((DEPTH, D_MODEL), 0.02)
    w_in = nrm((DEPTH, D_MODEL, P_TOT), D_MODEL ** -0.5)
    lin = jnp.linspace(ML_FGATE_LO, ML_FGATE_HI, ML_HEADS, dtype=f32)
    zh = jnp.zeros((ML_HEADS,), f32)
    fbias = jnp.concatenate([zh, lin, zh, lin])
    b_in = nrm((DEPTH, P_TOT), 0.02).at[:, OFF_MLG:OFF_GATE].add(fbias)
    hy_conv_w = nrm((DEPTH, 3, 3, P_HY), 1.0 / 3.0)
    hy_conv_b = nrm((DEPTH, P_HY), 0.02)
    hy_f_w1 = nrm((DEPTH, HY_POS_DIM, HY_FILTER_HID), HY_POS_DIM ** -0.5)
    hy_f_b1 = nrm((DEPTH, HY_FILTER_HID), 0.02)
    hy_f_w2 = nrm((DEPTH, HY_FILTER_HID, HY_FILTER_HID), HY_FILTER_HID ** -0.5)
    hy_f_b2 = nrm((DEPTH, HY_FILTER_HID), 0.02)
    hy_f_w3 = nrm((DEPTH, HY_FILTER_HID, HY_ORDER * 2 * D_BR), HY_FILTER_HID ** -0.5)
    hy_f_freq = 1.0 + nrm((DEPTH, HY_FILTER_HID), 0.02)
    decay_base = jnp.linspace(HY_DECAY_SLOW, HY_DECAY_FAST, D_BR, dtype=f32)
    hy_decay = decay_base[None, None, None, :] + nrm((DEPTH, HY_ORDER, 2, D_BR), 0.1)
    hy_skip = nrm((DEPTH, HY_ORDER, D_BR), 0.5)
    ml_conv_w = nrm((DEPTH, 3, 3, 2 * D_BR), 1.0 / 3.0)
    ml_conv_b = nrm((DEPTH, 2 * D_BR), 0.02)
    ml_norm_w = 1.0 + nrm((DEPTH, D_BR), 0.02)
    w_branch = nrm((DEPTH, N_BRANCH, D_BR, D_MODEL), D_BR ** -0.5)
    w_out = nrm((DEPTH, D_MODEL, D_MODEL), D_MODEL ** -0.5)
    moe_rg_w = nrm((DEPTH, D_MODEL, MOE_GROUPS), D_MODEL ** -0.5)
    moe_rg_b = nrm((DEPTH, MOE_GROUPS), 0.01)
    moe_re_w = nrm((DEPTH, D_MODEL, MOE_EXPERTS), D_MODEL ** -0.5)
    moe_re_b = nrm((DEPTH, MOE_EXPERTS), 0.01)
    moe_w_gate = nrm((DEPTH, MOE_EXPERTS, D_MODEL, EXPERT_HID), D_MODEL ** -0.5)
    moe_w_up = nrm((DEPTH, MOE_EXPERTS, D_MODEL, EXPERT_HID), D_MODEL ** -0.5)
    moe_w_down = nrm((DEPTH, MOE_EXPERTS, EXPERT_HID, D_MODEL), EXPERT_HID ** -0.5)
    norm_f_w = 1.0 + nrm((D_MODEL,), 0.02)
    return {"x": x, "c": c, "ctx": ctx, "c_ctx": c_ctx, "ada_w": ada_w, "ada_b": ada_b,
            "norm1_w": norm1_w, "norm2_w": norm2_w, "w_in": w_in, "b_in": b_in,
            "hy_conv_w": hy_conv_w, "hy_conv_b": hy_conv_b, "hy_f_w1": hy_f_w1, "hy_f_b1": hy_f_b1,
            "hy_f_w2": hy_f_w2, "hy_f_b2": hy_f_b2, "hy_f_w3": hy_f_w3, "hy_f_freq": hy_f_freq,
            "hy_decay": hy_decay, "hy_skip": hy_skip, "ml_conv_w": ml_conv_w, "ml_conv_b": ml_conv_b,
            "ml_norm_w": ml_norm_w, "w_branch": w_branch, "w_out": w_out,
            "moe_rg_w": moe_rg_w, "moe_rg_b": moe_rg_b, "moe_re_w": moe_re_w, "moe_re_b": moe_re_b,
            "moe_w_gate": moe_w_gate, "moe_w_up": moe_w_up, "moe_w_down": moe_w_down,
            "norm_f_w": norm_f_w}

def first_block(x, c, ctx, c_ctx, ada_w, ada_b, norm1_w, norm2_w, w_in, b_in,
              hy_conv_w, hy_conv_b, hy_f_w1, hy_f_b1, hy_f_w2, hy_f_b2, hy_f_w3, hy_f_freq,
              hy_decay, hy_skip, ml_conv_w, ml_conv_b, ml_norm_w, w_branch, w_out,
              moe_rg_w, moe_rg_b, moe_re_w, moe_re_b, moe_w_gate, moe_w_up, moe_w_down,
              norm_f_w):
    B = x.shape[0]
    rows = x.shape[1] // GRID_W
    lat_grid = (rows, GRID_W)
    ctx_grid = (1, ctx.shape[1])
    for l in range(DEPTH):
        lp = {"hy_conv_w": hy_conv_w[l], "hy_conv_b": hy_conv_b[l], "hy_f_w1": hy_f_w1[l],
              "hy_f_b1": hy_f_b1[l], "hy_f_w2": hy_f_w2[l], "hy_f_b2": hy_f_b2[l],
              "hy_f_w3": hy_f_w3[l], "hy_f_freq": hy_f_freq[l], "hy_decay": hy_decay[l],
              "hy_skip": hy_skip[l], "ml_conv_w": ml_conv_w[l], "ml_conv_b": ml_conv_b[l],
              "ml_norm_w": ml_norm_w[l], "w_branch": w_branch[l], "w_out": w_out[l],
              "moe_rg_w": moe_rg_w[l], "moe_rg_b": moe_rg_b[l], "moe_re_w": moe_re_w[l],
              "moe_re_b": moe_re_b[l], "moe_w_gate": moe_w_gate[l], "moe_w_up": moe_w_up[l],
              "moe_w_down": moe_w_down[l]}
        last = l == DEPTH - 1
        mod_l = jnp.split((jax.nn.silu(c) @ ada_w[l] + ada_b[l])[:, None, :], 6, axis=-1)
        mod_c = jnp.split((jax.nn.silu(c_ctx) @ ada_w[l] + ada_b[l])[None, None, :], 6, axis=-1)
        zc = modulate(rmsnorm(ctx, norm1_w[l]), mod_c[0], mod_c[1]) @ w_in[l] + b_in[l]
        zl = modulate(rmsnorm(x, norm1_w[l]), mod_l[0], mod_l[1]) @ w_in[l] + b_in[l]
        st0 = zero_state(B)
        ml_c, st_f, st_b = mlstm_branch(zc[..., OFF_ML:OFF_MLG], zc[..., OFF_MLG:OFF_GATE], ctx_grid, lp, st0, st0)
        ml_l, _, _ = mlstm_branch(zl[..., OFF_ML:OFF_MLG], zl[..., OFF_MLG:OFF_GATE], lat_grid, lp, st_f, st_b)
        x = x + mod_l[2] * token_mixer_out(zl, lat_grid, lp, ml_l)
        x = x + mod_l[5] * hier_moe(modulate(rmsnorm(x, norm2_w[l]), mod_l[3], mod_l[4]), lp)
        if not last:
            ctx = ctx + mod_c[2] * token_mixer_out(zc, ctx_grid, lp, ml_c)
            ctx = ctx + mod_c[5] * hier_moe(modulate(rmsnorm(ctx, norm2_w[l]), mod_c[3], mod_c[4]), lp)
    return rmsnorm(x, norm_f_w)


DEPTH_2 = 4

HEAD_DIM = 64
ROT_DIM = HEAD_DIM // 4
ROPE_THETA = 500000.0
N_MIXERS = 3
A_HEADS = D_MODEL // HEAD_DIM
A_KV_HEADS = 4
A_WINDOW = 128
WIN_BLK = 128
B_HEADS = D_MODEL // HEAD_DIM
B_GROUPS = ((128, 1), (512, 4), (2048, 16))
C_HEADS = D_MODEL // HEAD_DIM
MOBA_BLOCK = 256
MOBA_TOPK = 3
MOBA_QCHUNK = 16
D_FF = ((8 * D_MODEL + 3 * 256 - 1) // (3 * 256)) * 256
DN_ALPHA = (2 * DEPTH_2) ** 0.25
DN_BETA = (8 * DEPTH_2) ** -0.25
LN_EPS = 1e-5
NEG = -1e30


def layer_norm(x, g, b):
    xf = x.astype(jnp.float32)
    mu = xf.mean(-1, keepdims=True)
    var = jnp.square(xf - mu).mean(-1, keepdims=True)
    return ((xf - mu) * lax.rsqrt(var + LN_EPS) * g.astype(jnp.float32) + b.astype(jnp.float32)).astype(x.dtype)

def rope_tables(positions):
    inv = ROPE_THETA ** (-jnp.arange(0, ROT_DIM, 2, dtype=jnp.float32) / ROT_DIM)
    ang = positions.astype(jnp.float32)[..., None] * inv
    return jnp.cos(ang), jnp.sin(ang)

def apply_rope(x, cos, sin):
    xf = x.astype(jnp.float32)
    half = ROT_DIM // 2
    x1, x2 = xf[..., :half], xf[..., half:ROT_DIM]
    c, s = cos[:, :, None, :], sin[:, :, None, :]
    return jnp.concatenate([x1 * c - x2 * s, x2 * c + x1 * s, xf[..., ROT_DIM:]], axis=-1).astype(x.dtype)

def block_attention(q, k, v, blk, n_back, with_prev, sink=None):
    B, L, Hq, dh = q.shape
    Hkv = k.shape[2]
    G = Hq // Hkv
    nb = L // blk
    qb = q.astype(jnp.float32).reshape(B, nb, blk, Hkv, G, dh)
    kb = k.astype(jnp.float32).reshape(B, nb, blk, Hkv, dh)
    vb = v.astype(jnp.float32).reshape(B, nb, blk, Hkv, dh)
    if with_prev:
        shift = lambda t: jnp.pad(t, ((0, 0), (1, 0), (0, 0), (0, 0), (0, 0)))[:, :-1]
        kb = jnp.concatenate([shift(kb), kb], axis=2)
        vb = jnp.concatenate([shift(vb), vb], axis=2)
    off = blk if with_prev else 0
    nk = kb.shape[2]
    s = jnp.einsum('bnqhgd,bnkhd->bnhgqk', qb, kb) * (dh ** -0.5)
    diff = jnp.arange(blk)[:, None] + off - jnp.arange(nk)[None, :]
    ok = ((diff >= 0) & (diff <= n_back))[None]
    if with_prev:
        ok = ok & ((jnp.arange(nb)[:, None, None] > 0) | (jnp.arange(nk)[None, None, :] >= blk))
    s = jnp.where(ok[None, :, None, None], s, NEG)
    m = s.max(-1)
    if sink is not None:
        sk = sink.astype(jnp.float32).reshape(1, 1, Hkv, G, 1)
        m = jnp.maximum(m, sk)
    p = jnp.exp(s - m[..., None])
    l = p.sum(-1)
    if sink is not None:
        l = l + jnp.exp(sk - m)
    o = jnp.einsum('bnhgqk,bnkhd->bnqhgd', p, vb) / jnp.transpose(l, (0, 1, 4, 2, 3))[..., None]
    lse = jnp.transpose(m + jnp.log(l), (0, 1, 4, 2, 3)).reshape(B, L, Hq)
    return o.reshape(B, L, Hq, dh), lse

def mixer_a(x, w_qkv, b_qkv, sinks, w_o, b_o, cos, sin):
    B, S, _ = x.shape
    nq, nkv = A_HEADS * HEAD_DIM, A_KV_HEADS * HEAD_DIM
    qkv = x @ w_qkv + b_qkv
    q = apply_rope(qkv[..., :nq].reshape(B, S, A_HEADS, HEAD_DIM), cos, sin)
    k = apply_rope(qkv[..., nq:nq + nkv].reshape(B, S, A_KV_HEADS, HEAD_DIM), cos, sin)
    v = qkv[..., nq + nkv:].reshape(B, S, A_KV_HEADS, HEAD_DIM)
    o, _ = block_attention(q, k, v, WIN_BLK, A_WINDOW - 1, True, sinks)
    return o.reshape(B, S, nq).astype(x.dtype) @ w_o + b_o

def dilated_attention(q, k, v, window, dil):
    B, S, H, dh = q.shape
    span = dil * WIN_BLK
    S_pad = -(-S // span) * span
    L = S_pad // dil

    def to_phase(t):
        t = jnp.pad(t, ((0, 0), (0, S_pad - S), (0, 0), (0, 0)))
        return jnp.transpose(t.reshape(B, L, dil, H, dh), (0, 2, 1, 3, 4)).reshape(B * dil, L, H, dh)

    o, lse = block_attention(to_phase(q), to_phase(k), to_phase(v), WIN_BLK, window // dil, True)
    o = jnp.transpose(o.reshape(B, dil, L, H, dh), (0, 2, 1, 3, 4)).reshape(B, S_pad, H, dh)[:, :S]
    lse = jnp.transpose(lse.reshape(B, dil, L, H), (0, 2, 1, 3)).reshape(B, S_pad, H)[:, :S]
    return o, lse

def mixer_b(x, w_qkv, w_o, cos, sin):
    B, S, _ = x.shape
    qkv = (x @ w_qkv).reshape(B, S, len(B_GROUPS), 3, B_HEADS, HEAD_DIM)
    outs, lses = [], []
    for g, (window, dil) in enumerate(B_GROUPS):
        q = apply_rope(qkv[:, :, g, 0], cos, sin)
        k = apply_rope(qkv[:, :, g, 1], cos, sin)
        o, lse = dilated_attention(q, k, qkv[:, :, g, 2], window, dil)
        outs.append(o)
        lses.append(lse)
    w = jax.nn.softmax(jnp.stack(lses), axis=0)
    o = jnp.sum(w[..., None] * jnp.stack(outs), axis=0)
    return o.reshape(B, S, B_HEADS * HEAD_DIM).astype(x.dtype) @ w_o

def mixer_c(x, w_qkv, w_o, cos, sin):
    B, S, _ = x.shape
    H, dh = C_HEADS, HEAD_DIM
    qkv = (x @ w_qkv).reshape(B, S, 3, H, dh)
    q = apply_rope(qkv[:, :, 0], cos, sin)
    k = apply_rope(qkv[:, :, 1], cos, sin)
    v = qkv[:, :, 2]
    S_pad = -(-S // MOBA_BLOCK) * MOBA_BLOCK
    nblk = S_pad // MOBA_BLOCK
    pad = ((0, 0), (0, S_pad - S), (0, 0), (0, 0))
    q, k, v = jnp.pad(q, pad), jnp.pad(k, pad), jnp.pad(v, pad)
    o_self, lse_self = block_attention(q, k, v, MOBA_BLOCK, MOBA_BLOCK - 1, False)
    qf = q.astype(jnp.float32)
    kblk = k.reshape(B, nblk, MOBA_BLOCK, H, dh)
    vblk = v.reshape(B, nblk, MOBA_BLOCK, H, dh)
    kmean = kblk.astype(jnp.float32).mean(axis=2)
    gate = jnp.einsum('bshd,bnhd->bshn', qf, kmean)
    n_past = jnp.arange(S_pad) // MOBA_BLOCK
    gate = jnp.where((jnp.arange(nblk)[None, :] < n_past[:, None])[None, :, None, :], gate, NEG)
    topk = min(MOBA_TOPK, nblk)
    _, idx = lax.top_k(gate, topk)
    valid = jnp.arange(topk)[None, :] < n_past[:, None]
    kbt = jnp.transpose(kblk, (0, 3, 1, 2, 4))
    vbt = jnp.transpose(vblk, (0, 3, 1, 2, 4))
    nc = S_pad // MOBA_QCHUNK
    q_c = jnp.transpose(qf.reshape(B, nc, MOBA_QCHUNK, H, dh), (1, 0, 2, 3, 4))
    i_c = jnp.transpose(idx.reshape(B, nc, MOBA_QCHUNK, H, topk), (1, 0, 2, 3, 4))
    v_c = valid.reshape(nc, MOBA_QCHUNK, topk)
    bi = jnp.arange(B)[:, None, None, None]
    hi = jnp.arange(H)[None, None, :, None]
    scale = dh ** -0.5

    def chunk(args):
        qc, ic, vc = args
        kg = kbt[bi, hi, ic].astype(jnp.float32)
        vg = vbt[bi, hi, ic].astype(jnp.float32)
        s = jnp.einsum('bqhd,bqhjkd->bqhjk', qc, kg) * scale
        s = jnp.where(vc[None, :, None, :, None], s, NEG)
        m = s.max(axis=(-2, -1))
        p = jnp.exp(s - m[..., None, None])
        l = p.sum(axis=(-2, -1))
        o = jnp.einsum('bqhjk,bqhjkd->bqhd', p, vg) / l[..., None]
        return o, m + jnp.log(l)

    o_sel, lse_sel = lax.map(chunk, (q_c, i_c, v_c))
    o_sel = jnp.transpose(o_sel, (1, 0, 2, 3, 4)).reshape(B, S_pad, H, dh)
    lse_sel = jnp.transpose(lse_sel, (1, 0, 2, 3)).reshape(B, S_pad, H)
    m = jnp.maximum(lse_self, lse_sel)
    w1 = jnp.exp(lse_self - m)
    w2 = jnp.exp(lse_sel - m)
    o = (w1[..., None] * o_self + w2[..., None] * o_sel) / (w1 + w2)[..., None]
    return o[:, :S].reshape(B, S, H * dh).astype(x.dtype) @ w_o

def swiglu(x, w_gate_up, w_down):
    gu = x @ w_gate_up
    gate, up = gu[..., :D_FF], gu[..., D_FF:]
    return (jax.nn.silu(gate) * up) @ w_down

def second_inputs(seed: int = 0) -> dict:
    key = jax.random.key(seed)
    ks = jax.random.split(key, 16)
    n_a = (DEPTH_2 + 2) // 3
    n_b = (DEPTH_2 + 1) // 3
    n_c = DEPTH_2 // 3
    D = D_MODEL
    a_cols = (A_HEADS + 2 * A_KV_HEADS) * HEAD_DIM
    b_cols = len(B_GROUPS) * 3 * B_HEADS * HEAD_DIM
    c_cols = 3 * C_HEADS * HEAD_DIM
    nrm = lambda k, shape, fan_in, s=1.0: jax.random.normal(k, shape, jnp.float32) * (fan_in ** -0.5) * s
    return {
        "x": jax.random.normal(ks[0], (BATCH, SEQ, D), jnp.float32),
        "positions": jnp.broadcast_to(jnp.arange(SEQ, dtype=jnp.int32), (BATCH, SEQ)),
        "ln_g": 1.0 + 0.02 * jax.random.normal(ks[1], (DEPTH_2, 2, D), jnp.float32),
        "ln_b": 0.02 * jax.random.normal(ks[2], (DEPTH_2, 2, D), jnp.float32),
        "a_w_qkv": nrm(ks[3], (n_a, D, a_cols), D),
        "a_b_qkv": 0.02 * jax.random.normal(ks[4], (n_a, a_cols), jnp.float32),
        "a_sinks": 0.5 * jax.random.normal(ks[5], (n_a, A_HEADS), jnp.float32),
        "a_w_o": nrm(ks[6], (n_a, A_HEADS * HEAD_DIM, D), A_HEADS * HEAD_DIM, DN_BETA),
        "a_b_o": 0.02 * jax.random.normal(ks[7], (n_a, D), jnp.float32),
        "b_w_qkv": nrm(ks[8], (n_b, D, b_cols), D),
        "b_w_o": nrm(ks[9], (n_b, B_HEADS * HEAD_DIM, D), B_HEADS * HEAD_DIM, DN_BETA),
        "c_w_qkv": nrm(ks[10], (n_c, D, c_cols), D),
        "c_w_o": nrm(ks[11], (n_c, C_HEADS * HEAD_DIM, D), C_HEADS * HEAD_DIM, DN_BETA),
        "w_gate_up": nrm(ks[12], (DEPTH_2, D, 2 * D_FF), D),
        "w_down": nrm(ks[13], (DEPTH_2, D_FF, D), D_FF, DN_BETA),
    }

def second_block(x, positions, ln_g, ln_b, a_w_qkv, a_b_qkv, a_sinks, a_w_o, a_b_o,
              b_w_qkv, b_w_o, c_w_qkv, c_w_o, w_gate_up, w_down):
    cos, sin = rope_tables(positions)
    for i in range(DEPTH_2):
        kind, j = i % N_MIXERS, i // N_MIXERS
        if kind == 0:
            h = mixer_a(x, a_w_qkv[j], a_b_qkv[j], a_sinks[j], a_w_o[j], a_b_o[j], cos, sin)
        elif kind == 1:
            h = mixer_b(x, b_w_qkv[j], b_w_o[j], cos, sin)
        else:
            h = mixer_c(x, c_w_qkv[j], c_w_o[j], cos, sin)
        x = layer_norm(DN_ALPHA * x + h, ln_g[i, 0], ln_b[i, 0])
        x = layer_norm(DN_ALPHA * x + swiglu(x, w_gate_up[i], w_down[i]), ln_g[i, 1], ln_b[i, 1])
    return x


def setup_inputs(seed=0):
    out = dict(first_inputs(seed))
    for name, value in second_inputs(seed + 1).items():
        if name != "x":
            out[name + "_2"] = value
    return out


def reference(
    x, c, ctx, c_ctx, ada_w, ada_b, norm1_w, norm2_w, w_in, b_in, hy_conv_w, hy_conv_b, hy_f_w1,
    hy_f_b1, hy_f_w2, hy_f_b2, hy_f_w3, hy_f_freq, hy_decay, hy_skip, ml_conv_w, ml_conv_b,
    ml_norm_w, w_branch, w_out, moe_rg_w, moe_rg_b, moe_re_w, moe_re_b, moe_w_gate, moe_w_up,
    moe_w_down, norm_f_w, positions_2, ln_g_2, ln_b_2, a_w_qkv_2, a_b_qkv_2, a_sinks_2, a_w_o_2,
    a_b_o_2, b_w_qkv_2, b_w_o_2, c_w_qkv_2, c_w_o_2, w_gate_up_2, w_down_2,
):
    x = first_block(
        x, c, ctx, c_ctx, ada_w, ada_b, norm1_w, norm2_w, w_in, b_in, hy_conv_w, hy_conv_b,
        hy_f_w1, hy_f_b1, hy_f_w2, hy_f_b2, hy_f_w3, hy_f_freq, hy_decay, hy_skip, ml_conv_w,
        ml_conv_b, ml_norm_w, w_branch, w_out, moe_rg_w, moe_rg_b, moe_re_w, moe_re_b,
        moe_w_gate, moe_w_up, moe_w_down, norm_f_w,
    )
    return second_block(
        x, positions_2, ln_g_2, ln_b_2, a_w_qkv_2, a_b_qkv_2, a_sinks_2, a_w_o_2, a_b_o_2,
        b_w_qkv_2, b_w_o_2, c_w_qkv_2, c_w_o_2, w_gate_up_2, w_down_2,
    )


_drawn_inputs = setup_inputs


def setup_inputs(seed=0):
    import zlib

    import numpy as np

    out = dict(_drawn_inputs(seed))
    spreads = {}
    factors = {'ctx': 2.785,
     'norm1_w': 4.104,
     'norm2_w': 7.248,
     'hy_conv_b': 2.965,
     'hy_f_b1': 2.986,
     'hy_f_freq': 4.635,
     'ml_conv_b': 64.0,
     'ml_norm_w': 84.175,
     'moe_rg_b': 64.0,
     'moe_re_b': 49.858,
     'a_b_qkv_2': 7.484,
     'a_sinks_2': 8.0,
     'a_b_o_2': 3.163}
    for name, (base, spread) in spreads.items():
        noise = np.random.default_rng([zlib.crc32(name.encode()), seed]).standard_normal(out[name].shape)
        drawn = base * np.exp(spread * noise) if base else spread * noise
        out[name] = __import__('jax').numpy.asarray(drawn.astype(out[name].dtype))
    for name, factor in factors.items():
        out[name] = (out[name] * factor).astype(out[name].dtype)
    return out
```

```python
from contextlib import ExitStack

import numpy as np

import concourse.bass as bass
from concourse import mybir

F32 = mybir.dt.float32
F32R = mybir.dt.float32r
I32 = mybir.dt.int32
ACT = mybir.ActivationFunctionType
ALU = mybir.AluOpType
AX = mybir.AxisListType.X

P = 128
D = 1024
KT = D // P
T = 256
TT = T // P
DB = 512
BT = DB // P
MLH = 4
EXPERTS = 16
HD = 64
HEADS = 16
FF = 2816
NFF = FF // T
LAYERS = 4
KINDS = (0, 1, 2, 0)
GROUPS = {0: 1, 1: 3, 2: 1}
MASK_OF = {0: (0,), 1: (1, 2, 3), 2: (4,)}
ALPHA = (2 * LAYERS) ** 0.25
NEG = -1e30
UNIT = KT * P
CHUNK = 4
NCHUNK = 3
NRAW = CHUNK * NCHUNK
NSPLIT = 3
EPS_RMS = 1e-6
EPS_LN = 1e-5
TWO_PI = 2 * np.pi

VECS = [("c", 16), ("ada_b", 48), ("norm1_w", 8), ("norm2_w", 8), ("norm_f_w", 8), ("b_in", 52),
        ("hy_conv_w", 108), ("hy_conv_b", 12), ("ml_conv_w", 72), ("ml_conv_b", 8), ("hy_skip", 8),
        ("ml_norm_w", 4), ("ln_g", 64), ("ln_b", 64), ("a_bq", 16), ("a_bk", 8), ("a_bo", 16)]
VOFF, _n = {}, 0
for _name, _c in VECS:
    VOFF[_name] = _n
    _n += _c
NVEC = _n
ROWS = [("b_v", DB), ("b_gates", 16), ("b_route", 20), ("a_bv", 2 * T)]
ROFF, _n = {}, 0
for _name, _c in ROWS:
    ROFF[_name] = _n
    _n += _c
NROW = _n
CONSTS = [("ident", P), ("flip", P), ("rot", P), ("fn_c", 2 * P), ("freq", 1), ("tcol", 2), ("drop0", 2)]
COFF, _n = {}, 0
for _name, _c in CONSTS:
    COFF[_name] = _n
    _n += _c
NCONST = _n


def plan():
    units = [("ada", i) for i in range(48)]
    units += [("in", i) for i in range(56)]
    units += [("branch", i) for i in range(12)] + [("out", i) for i in range(8)]

    def ffn(what, n):
        for i in range(n + 1):
            if i < n:
                for part in ("gate0", "up0", "gate1", "up1"):
                    yield what, i, part
            if i:
                for part in ("down0", "down1"):
                    yield what, i - 1, part

    units += list(ffn("expert", EXPERTS))
    for layer, kind in enumerate(KINDS):
        for quad in range(4):
            if kind == 0:
                parts = [("k", 0)] + [("v", 0), ("v", 1)] * (quad == 0) + [("q", 0), ("q", 1)]
            else:
                parts = [(part, 2 * g + i) for g in range(GROUPS[kind]) for part in "vkq" for i in range(2)]
            units += [("qkv", layer, quad, *part) for part in parts]
        units += [("wo", layer, i) for i in range(8)]
        units += list(ffn(("ffn", layer), NFF))
    return units


def build_program(nc, a, out):
    units = plan()
    first = {}
    for n, u in enumerate(units):
        first.setdefault(u[0:2] if u[0] in ("qkv", "wo") else u[0], n)
    split0 = first["expert"]
    chunks = -(-len(units) // CHUNK)

    with ExitStack() as ctx:
        def sb(name, shape, dt=F32):
            return ctx.enter_context(nc.sbuf_tensor(name, shape, dt))

        def pb(name, shape):
            return ctx.enter_context(nc.psum_tensor(name, shape, F32))

        def alias(name, shape, base, offset, dt=F32R):
            return nc.alloc_sbuf_tensor_at(name, shape, dt, offset=base + 4 * offset)

        ring = sb("ring", [P, NRAW, UNIT])
        wsplit = sb("wsplit", [P, NSPLIT, 2, UNIT], F32R)
        consts = sb("consts", [P, NCONST])
        vecs = sb("vecs", [P, NVEC])
        rows = sb("rows", [1, NROW])
        ones = sb("ones", [P, P])
        mean_w = sb("mean_w", [P, P])
        x = sb("x", [P, KT, T])
        cx = sb("cx", [P, KT, T])
        rh = sb("rh", [P, 4096])
        rh_at = nc.sbuf_base - 4 * 4096
        rs = sb("rs", [P, 4096])
        rs_at = nc.sbuf_base - 4 * 4096
        ar = sb("ar", [P, 16400])
        ar_at = nc.sbuf_base - 4 * 16400
        nrm = sb("nrm", [P, 3, 512])
        ropes = sb("ropes", [P, 2, T])
        modv = sb("modv", [P, 48, 2])
        cs = sb("cs", [P, 16])
        gain = sb("gain", [P, 8, 3])
        hyf = sb("hyf", [64, 3])
        hyh2 = sb("hyh2", [64, T])
        wg16 = sb("wg16", [P, KT, 16])
        wr20 = sb("wr20", [P, KT, 20])
        sinks = sb("sinks", [P, 32])
        zp = sb("zp", [P, 4, 4, 8])
        ct = sb("ct", [P, 8, 8])
        cb = sb("cb", [P, 8, 4])
        ecol = sb("ecol", [P, 2, 2, 4])
        rb = sb("rb", [4, T])
        small = sb("small", [P, 256])

        ident = consts[:, COFF["ident"]:COFF["ident"] + P]
        flip = consts[:, COFF["flip"]:COFF["flip"] + P]
        rot = consts[:, COFF["rot"]:COFF["rot"] + P]
        fn_c = consts[:, COFF["fn_c"]:COFF["fn_c"] + 2 * P]

        def vec(name, i=0):
            return vecs[:, VOFF[name] + i:VOFF[name] + i + 1]

        def row(name, lo, n):
            return rows[0:1, ROFF[name] + lo:ROFF[name] + lo + n]

        pg = [pb(f"pg{i}", [P, 512]) for i in range(2)]
        pd = pb("pd", [P, 4, 512])
        pm = [pb(f"pm{i}", [P, 512]) for i in range(2)]

        g_sig = ar[:, 0:6144].rearrange("p (m t) -> p m t", t=T)
        hyc = ar[:, 6144:9216].rearrange("p (m t) -> p m t", t=T)
        qf = ar[:, 9216:10240].rearrange("p (m t) -> p m t", t=T)
        kf = ar[:, 10240:11264].rearrange("p (m t) -> p m t", t=T)
        kc = ar[:, 11264:12288].rearrange("p (m t) -> p m t", t=T)
        vx = ar[:, 12288:14352].rearrange("p (s h v) -> p s h v", s=4, v=P + 1)
        zfn = ar[:, 14352:15376].rearrange("p (m t) -> p m t", t=T)
        osig = ar[:, 15376:16400].rearrange("p (m t) -> p m t", t=T)
        hc = rh[:, :].rearrange("p (k t) -> p k t", k=KT)
        h1 = ar[:, 4096:6144].rearrange("p (k t) -> p k t", k=KT)
        sq2 = rs[:, :].rearrange("p (k t) -> p k t", k=KT)
        sq1 = rs[:, 0:2048].rearrange("p (k t) -> p k t", k=KT)
        zring = rs[:, 0:3168].rearrange("p (n r c) -> p n r c", n=8, c=66)
        kpad = rs[:, 3168:3684].rearrange("p (n c) -> p n c", n=2)
        cxf = cx[:, :, :].rearrange("p k t -> p (k t)")
        fn_l = cxf[:, 0:1024].rearrange("p (f s t) -> p f s t", f=2, s=TT)
        mlmask = cxf[:, 1024:2048].rearrange("p (d s t) -> p d s t", d=2, s=TT)
        hyh = ar[0:64, 0:1024].rearrange("p (n t) -> p n t", n=4)
        feat = ar[0:33, 1024:1280]
        hyw = ar[0:64, 1280:1408]
        posi = ar[:, 1408:1664].bitcast(I32)
        mod_row = ar[0:2, 6144:12288]
        dft = cxf[:, 0:1536].rearrange("p (s f) -> p s f", s=TT)
        idft = (cxf[:, 1536:1792], cxf[:, 1792:2048], rs[:, 3584:3840], rs[:, 3840:4096])
        masks = cxf[:, 0:1920].rearrange("p (n k) -> p n k", n=5)
        qks = rh[:, 0:1024].rearrange("p (s t) -> p s t", s=4)
        wexp = rh[:, 1024:1536].rearrange("p (n t) -> p n t", n=2)
        wtmp = rh[:, 1536:2048].rearrange("p (n t) -> p n t", n=2)
        smat = rh[:, 2048:2560].rearrange("p (n t) -> p n t", n=2)
        negm = rh[:, 3584:4096]
        hml = rh[:, 2560:3584].rearrange("p (t h v) -> p t h v", t=2, v=P)
        rr = rs[0:8, 0:3584].rearrange("p (n t) -> p n t", n=7)
        fnp = rs[:, 0:1024].rearrange("p (n t) -> p n t", n=2)
        hk = rh[:, 0:2048].rearrange("p (s d c) -> p s d c", s=2, d=2)
        hdec = rh[:, 2048:4096].rearrange("p (s n) -> p s n", s=2)
        kfr = rs[:, 0:2560].rearrange("p (n c) -> p n c", n=5)
        ptmp = rs[:, 2560:3584].rearrange("p (n c) -> p n c", n=2)
        w3 = ar[0:64, 9216:11264]
        utok = ar[:, 11264:12288].rearrange("p (s c) -> p s c", s=2)
        yfr = ar[:, 12288:14336].rearrange("p (f c) -> p f c", f=4)
        mix = rh[:, 0:2048].rearrange("p (k t) -> p k t", k=KT)
        mtmp = rs[:, 0:512].rearrange("p (n t) -> p n t", n=2)
        comb = ar[:, 0:4096].rearrange("p (e t) -> p e t", e=EXPERTS)
        silu_g = rs[:, 2048:2560].rearrange("p (m t) -> p m t", m=2)
        utmp = rs[:, 2560:3072].rearrange("p (m t) -> p m t", m=2)
        htmp = rs[:, 3072:3584].rearrange("p (m t) -> p m t", m=2)
        route = rs[:, 3584:3744]
        combine = rs[:, 3744:3776]
        cmt = rs[0:16, 3776:4032]
        xs = alias("xs", [P, 2, KT, T], rh_at, 0)
        hid = alias("hid", [P, 2, 2, 2, T], rs_at, 0)
        otl = alias("otl", [P, KT, T], rs_at, 0)
        oth = alias("oth", [P, KT, T], ar_at, 14088)
        s0 = ar[:, 0:1540].rearrange("p (h k) -> p h k", h=4)
        s1 = ar[:, 1540:4616].rearrange("p (h k) -> p h k", h=4)
        qr = ar[:, 4616:6152].rearrange("p (g m t) -> p g m t", g=3, m=2)
        kr = ar[:, 6152:7688].rearrange("p (g m t) -> p g m t", g=3, m=2)
        vt = ar[:, 7688:10760].rearrange("p (n g s c) -> p n g s c", n=2, g=3, s=2)
        pt = ar[:, 10760:11528].rearrange("p (n k) -> p n k", n=2)
        raw = ar[:, 11528:12552].rearrange("p (n m t) -> p n m t", n=2, m=2)
        rt = ar[:, 12552:13576].rearrange("p (n m t) -> p n m t", n=2, m=2)
        osb = ar[:, 13576:14088].rearrange("p (q h d) -> p q h d", q=2, h=4)
        smx = small[:, 0:32].rearrange("p (n q h) -> p n q h", n=4, q=2)
        ml_ss, ml_y, ml_t, ml_ve = (small[:, 64 + 8 * i:72 + 8 * i] for i in range(4))
        ml_den, ml_rl = small[:, 96:98], small[:, 98:100]
        hy_ve, hy_rk, hy_t = (small[:, 104 + 8 * i:112 + 8 * i] for i in range(3))

        sems = {}

        def S(name):
            if name not in sems:
                sems[name] = ctx.enter_context(nc.semaphore(name))
            return sems[name]

        for name in SEMAPHORES:
            S(name)
        landed = [ctx.enter_context(nc.semaphore(f"chunk{i}_landed")) for i in range(NCHUNK)]

        def await_chunk(eng, c):
            eng.wait_ge(landed[c % NCHUNK], 16 * (c // NCHUNK + 1))

        def chunk_units(c):
            lo = CHUNK * (c % NCHUNK)
            return ring[:, lo:lo + CHUNK, :].rearrange("p b (k c) -> p b k c", c=P)

        ada0, in0, br0, wo0 = (first[n] // CHUNK for n in ("ada", "in", "branch", "out"))

        block = ctx.enter_context(nc.Block())

        @block.sync
        def _(sp):
            for c in range(chunks):
                if c >= NCHUNK:
                    last = c - NCHUNK
                    if CHUNK * last < split0:
                        sp.wait_ge(S("chunk_used"), last + 1)
                    else:
                        sp.wait_ge(S("low_done"), CHUNK * (last + 1) - split0)
                n = min(CHUNK, len(units) - CHUNK * c)
                lo = CHUNK * (c % NCHUNK)
                sp.dma_start(ring[:, lo:lo + n, :],
                             a["wstream"][c * CHUNK * P * UNIT:(c * CHUNK + n) * P * UNIT].rearrange(
                                 "(p u f) -> p u f", p=P, f=UNIT)).then_inc(landed[c % NCHUNK], 16)
            sp.wait_ge(S("x_full"), 8 * (2 + 2 * LAYERS))
            sp.dma_start(out.rearrange("(k p) t -> p k t", p=P), x[:, :, :]).then_inc(S("stored"), 16)
            sp.wait_ge(S("stored"), 16)

        @block.gpsimd
        def _(gp):
            gp.memset(ones[:, :], 1.0)
            gp.memset(mean_w[:, :], 1.0 / D)
            gp.memset(zp[:, :, :, :], 0.0)
            gp.memset(vx[:, :, :, P:P + 1], 1.0).then_inc(S("constants"), 1)
            gp.wait_ge(S("nrm_var"), 1)
            gp.memset(rs[:, 0:3684], 0.0).then_inc(S("pads_zero"), 1)
            gp.wait_ge(S("nrm_scaled"), 2)
            gp.dma_start(cxf, a["cx_tables"]).then_inc(S("cx_tables"), 16)
            gp.wait_ge(S("smat_used"), 32)
            gp.dma_start(w3, a["hy_w3"]).then_inc(S("w3_landed"), 16)
            gp.wait_ge(S("fn_out"), BT)
            gp.dma_start(cxf, a["dft_tables"][:, 0:2048]).then_inc(S("dft_landed"), 16)
            gp.dma_start(rs[:, 3584:4096], a["dft_tables"][:, 2048:2560]).then_inc(S("dft_landed"), 16)
            for o in range(2):
                if o:
                    gp.wait_ge(S("hy_energy"), o)
                for s in range(2):
                    gp.dma_start(hdec[:, s, :], a["hy_decay"][o * 1024:(o + 1) * 1024].partition_broadcast(P)
                                 ).then_inc(S("decay_landed"), 16)
            gp.wait_ge(S("hy_back"), 2)
            gp.dma_start(cxf[:, 0:1920], a["masks"]).then_inc(S("masks_landed"), 16)
            gp.wait_ge(S("masks_landed"), 16)

        @block.tensor
        def _(pe):
            held = [""]

            def mm(dst, lhs, rhs, start, stop, skip=False):
                ins = nc.tensor.matmul(dst, lhs, rhs, start=start, stop=stop, skip_group_check=skip)
                if held[0] == "two_used":
                    ins.then_inc(S("unit_used"), 2)
                    held[0] = ""
                elif held[0]:
                    ins.then_inc(S(held[0]), 1)
                    held[0] = ""
                return ins

            def use(c):
                await_chunk(pe, c)
                return chunk_units(c)

            def used(what="chunk_used"):
                assert not held[0]
                held[0] = what

            at = [split0]

            def unit(k_tiles=KT):
                n = at[0]
                at[0] += 1
                pe.wait_ge(S("low_done"), n - split0 + 1)
                w = wsplit[:, (n - split0) % NSPLIT, :, :]
                return [w[:, i, :].rearrange("p (k c) -> p k c", k=k_tiles) for i in range(2)]

            def three_pass(dst, lhs, rhs, nk=KT, k_wait=None, more=False):
                for k in range(nk):
                    if k_wait is not None:
                        pe.wait_ge(S("x_ready"), k_wait + k + 1)
                    for i, (l, r) in enumerate(((0, 0), (0, 1), (1, 0))):
                        last = mm(dst, lhs(l, k), rhs(r, k), k == 0 and i == 0,
                                  k == nk - 1 and i == 2 and not more)
                return last

            def product(dst, lhs, rhs, nk=KT):
                for k in range(nk):
                    last = mm(dst, lhs(k), rhs(k), k == 0, k == nk - 1)
                return last

            pe.wait_ge(S("loaded"), 16 * NLOADS)
            pe.wait_ge(S("constants"), 1)
            mm(pg[0][0:64, 0:T], hyw[0:33, 0:64], feat, True, True).then_inc(S("hy_net"), 1)
            pe.wait_ge(S("hy_sin"), 1)
            mm(pg[1][0:64, 0:T], hyw[:, 64:128], hyh[:, 3, :], True, True).then_inc(S("hy_net"), 1)

            pe.wait_ge(S("c_silu"), 1)
            cs2 = cs[:, :].rearrange("p (j k) -> p k j", j=2)
            for j in range(12):
                w = use(ada0 + j)
                if j >= 2:
                    pe.wait_ge(S("mod_row"), j - 1)
                for k in range(KT):
                    last = mm(pg[j % 2][0:2, :], cs2[:, k, :], w[:, :, k, :], k == 0, k == KT - 1)
                last.then_inc(S("mod_done"), 1)
                used()
            pe.wait_ge(S("mod_row"), 12)
            for f in range(48):
                last = mm(pm[0][:, 2 * f:2 * f + 2], mod_row[:, f * P:(f + 1) * P], ident[0:2, 0:2], True, True)
            last.then_inc(S("mod_raw"), 1)

            def spread_sum(dst, src):
                for k in range(KT):
                    last = mm(dst, mean_w[:, :], src(k), k == 0, k == KT - 1)
                return last

            def norm_sums(n, layer_norm):
                if layer_norm:
                    for k in range(KT):
                        pe.wait_ge(S("res_ready"), 8 * (n - 1) + k + 1)
                        last = mm(pm[0][:, 0:T], mean_w[:, :], x[:, k, :], k == 0, k == KT - 1)
                    last.then_inc(S("ln_mean"), 1)
                for k in range(KT):
                    if k % 2 == 0:
                        pe.wait_ge(S("nrm_sq"), 4 * n - 2 + k // 2 + 1)
                    last = mm(pm[1][:, 0:T], mean_w[:, :], sq1[:, k, :], k == 0, k == KT - 1)
                last.then_inc(S("nrm_var"), 1)

            pe.wait_ge(S("nrm_sq"), 2)
            spread_sum(pm[1][:, :], lambda k: sq2[:, k, :]).then_inc(S("nrm_var"), 1)

            pe.wait_ge(S("h_ready"), 16)
            job = [0]

            def bank():
                j = job[0]
                if j >= 2:
                    pe.wait_ge(S("in_out"), j - 1)
                job[0] += 1
                return pg[j % 2]

            w = use(in0)
            for s in range(4):
                p = bank()
                for k in range(KT):
                    mm(p[:, :], hc[:, k, s * P:(s + 1) * P], w[:, :, k, :], k == 0, False)
                mm(p[:, :], ones[0:1, :], row("b_v", 0, DB), False, True).then_inc(S("in_done"), 1)
            used()
            w = use(in0 + 1)
            for b in range(4):
                p = bank()
                product(p[:, :], lambda k: w[:, b, k, :], lambda k: hc[:, k, :]).then_inc(S("in_done"), 1)
            used()
            for s in range(4):
                for k in range(KT):
                    mm(pm[0][:, s * 16:(s + 1) * 16], hc[:, k, s * P:(s + 1) * P], wg16[:, k, :], k == 0, False)
                last = mm(pm[0][:, s * 16:(s + 1) * 16], ones[0:1, :], row("b_gates", 0, 16), False, True)
            last.then_inc(S("gates_raw"), 1)
            for c in range(2, 14):
                w = use(in0 + c)
                for b in (0, 2):
                    p = bank()
                    for i in range(2):
                        last = product(p[:, i * T:(i + 1) * T], lambda k: w[:, b + i, k, :],
                                       lambda k: hc[:, k, 0:T])
                    last.then_inc(S("in_done"), 1)
                used()

            pe.wait_ge(S("zp_ready"), 1)
            for r, dst in ((0, pm[1]), (1, pm[0])):
                for j in range(4):
                    fwd, bwd = (2, 3, 0, 1)[j], (3, 2, 1, 0)[j]
                    mm(dst[0:8, j * P:(j + 1) * P], zp[:, r, fwd, :], ident, True, False)
                    last = mm(dst[0:8, j * P:(j + 1) * P], zp[:, 2 + r, bwd, :], flip, False, True)
            last.then_inc(S("gate_rows"), 1)
            pe.wait_ge(S("rows_done"), 1)
            for j in range(4):
                mm(pm[1][:, j * 8:(j + 1) * 8], rr[:, 3, j * P:(j + 1) * P], ident[0:8, 0:8], True, True)
            for i in range(4):
                last = mm(pm[1][:, (4 + i) * 8:(5 + i) * 8], rr[:, 5 + i // 2, (2 + i % 2) * P:(3 + i % 2) * P],
                          ident[0:8, 0:8], True, True)
            last.then_inc(S("gate_cols"), 1)
            pe.wait_ge(S("ct_ready"), 1)
            mm(pm[0][:, 0:32], flip, ct[:, :, 4:8], True, True).then_inc(S("gate_back"), 1)
            pe.wait_ge(S("cb_ready"), 1)
            mm(pm[1][0:4, 0:P], cb[:, 5, :], ident, True, True)
            mm(pm[1][0:4, P:T], cb[:, 4, :], ident, True, True).then_inc(S("back_rows"), 1)
            pe.wait_ge(S("rb_ready"), 1)
            pe.wait_ge(S("qk_silu"), 1)
            for h in range(MLH):
                if h:
                    pe.wait_ge(S("qk_out"), h)
                for s in range(4):
                    keys = kf[:, h, s * P:(s + 1) * P] if s < 2 else kc[:, h, (s - 2) * P:(s - 1) * P]
                    mm(pd[:, s // 2, (s % 2) * T:(s % 2 + 1) * T], keys, qf[:, h, :], True, True)
                if h:
                    pe.wait_ge(S("wexp_done"), 8 * h)
                pick = ident[0:4, h:h + 1].to_broadcast([4, P])
                mm(pm[0][:, 0:T], pick, rr[0:4, 5, T:2 * T], True, True)
                mm(pm[0][:, T:2 * T], pick, rb[:, :], True, True).then_inc(S("qk_done"), 1)
                for d in range(2):
                    if h:
                        pe.wait_ge(S("ml_evac"), 2 * h + d - 1)
                    for i in range(4):
                        s = (2, 3, 0, 1)[i]
                        pe.wait_ge(S("smat_done"), 8 * h + 4 * d + i + 1)
                        for t in range(2):
                            last = mm((pd[:, 2 + t, 0:P + 1], pg[t][:, 0:P + 1])[d], smat[:, i % 2, t * P:(t + 1) * P],
                                      vx[:, s, h, :], i == 0, i == 3)
                        last.then_inc(S("smat_used"), 1)
            pe.wait_ge(S("hml_scaled"), 1)
            for h in range(MLH):
                for t in range(2):
                    last = nc.tensor.transpose(pd[:, h // 2, (h % 2) * T + t * P:(h % 2) * T + (t + 1) * P],
                                               hml[:, t, h, :], ident)
            last.then_inc(S("hml_read"), 1)

            pe.wait_ge(S("cx_tables"), 16)
            for g in range(BT):
                if g >= 2:
                    pe.wait_ge(S("fn_p"), g - 1)
                for t in range(TT):
                    last = mm(pg[g % 2][:, t * T:(t + 1) * T], zfn[:, g, t * P:(t + 1) * P], fn_c, True, True)
                last.then_inc(S("fn_first"), 1)
                pe.wait_ge(S("fn_p"), g + 1)
                if g >= 2:
                    pe.wait_ge(S("fn_out"), g - 1)
                for i in range(4):
                    f, t = i // 2, i % 2
                    last = mm(pm[g % 2][:, 0:T], fnp[:, g % 2, t * T + f * P:t * T + (f + 1) * P],
                              fn_l[:, f, t, :], i == 0, i == 3)
                last.then_inc(S("fn_second"), 1)

            pe.wait_ge(S("w3_landed"), 16)
            pe.wait_ge(S("fn_out"), BT)
            pe.wait_ge(S("y_ml"), 1)
            pe.wait_ge(S("hy_sin"), 2)
            for o in range(2):
                for t in range(TT):
                    for side in range(2):
                        last = mm(pd[:, 2 * t + side, :], hyh2[:, t * P:(t + 1) * P],
                                  w3[:, (2 * o + side) * DB:(2 * o + side + 1) * DB], True, True)
                last.then_inc(S("hy_taps"), 1)
                pe.wait_ge(S("hy_tapsq"), o + 1)
                for c in range(BT):
                    for i in range(4):
                        last = mm(pm[0][:, 4 * o + c:4 * o + c + 1],
                                  hdec[:, i // 2, (i % 2) * DB + c * P:(i % 2) * DB + (c + 1) * P],
                                  ones[:, 0:1], i == 0, i == 3)
                last.then_inc(S("hy_energy"), 1)
                pe.wait_ge(S("hy_sides"), o + 1)
                pe.wait_ge(S("dft_landed"), 32)
                for m in range(5):
                    if m >= 2:
                        pe.wait_ge(S("hy_specout"), 5 * o + m - 1)
                    f = (0, 1, 4, 3, 5)[m]
                    for t in range(TT):
                        last = mm(pg[m % 2][:, :], dft[:, t, f * P:(f + 1) * P], hk[:, t, int(m in (2, 3)), :],
                                  t == 0, t == 1)
                    last.then_inc(S("hy_spec"), 1)
                for t in range(TT):
                    for c in range(BT):
                        last = nc.tensor.transpose(pd[:, t, c * P:(c + 1) * P],
                                                   hyc[:, 4 * o + c, t * P:(t + 1) * P], ident)
                last.then_inc(S("hy_turned"), 1)
                pe.wait_ge(S("hy_utok"), o + 1)
                for m in range(4):
                    for t in range(TT):
                        last = mm(pd[:, m, :], dft[:, t, m * P:(m + 1) * P], utok[:, t, :], t == 0, t == 1)
                last.then_inc(S("hy_fwd"), 1)
                pe.wait_ge(S("hy_prod"), o + 1)
                for c in range(BT):
                    for m in range(4):
                        last = mm(pg[c // 2][:, (c % 2) * T:(c % 2 + 1) * T], yfr[:, m, c * P:(c + 1) * P],
                                  idft[m], m == 0, m == 3)
                last.then_inc(S("hy_back"), 1)
                pe.wait_ge(S("hy_z"), o + 1)

            for m in range(KT):
                if m >= 2:
                    pe.wait_ge(S("mixed"), m - 1)
                for b in range(3):
                    n = 3 * m + b
                    if n % (2 * CHUNK) == 0:
                        if n:
                            used()
                        w = use(br0 + n // (2 * CHUNK)).rearrange("p b (h k) c -> p (b h) k c", h=2)
                    dst = pd[:, 2 * (m % 2) + b // 2, (b % 2) * T:(b % 2 + 1) * T]
                    y = (hyc[:, 8:12, :], zfn, osig)[b]
                    last = product(dst, lambda k: w[:, n % (2 * CHUNK), k, :], lambda k: y[:, k, :], nk=BT)
                last.then_inc(S("branched"), 1)
            used()

            pe.wait_ge(S("mixed"), KT)
            for j in range(4):
                if j % 2 == 0:
                    w = use(wo0 + j // 2)
                if j >= 2:
                    pe.wait_ge(S("res_ready"), 2 * (j - 1))
                for i in range(2):
                    last = product(pg[j % 2][:, i * T:(i + 1) * T], lambda k: w[:, 2 * (j % 2) + i, k, :],
                                   lambda k: mix[:, k, :])
                last.then_inc(S("square_done"), 1)
                if j % 2:
                    used()
            norm_sums(1, False)

            pe.wait_ge(S("x_ready"), KT)
            for s in range(TT):
                for k in range(KT):
                    mm(pm[0][:, s * 20:(s + 1) * 20], h1[:, k, s * P:(s + 1) * P], wr20[:, k, :], k == 0, False)
                last = mm(pm[0][:, s * 20:(s + 1) * 20], ones[0:1, :], row("b_route", 0, 20), False, True)
            last.then_inc(S("logits"), 1)

            def ffn_up(u, k_wait=None):
                for m in range(2):
                    if u:
                        pe.wait_ge(S("hid_raw"), 2 * (u - 1) + m + 1)
                    for b in range(2):
                        w = unit()
                        last = three_pass(pg[m][:, b * T:(b + 1) * T], lambda i, k: w[i][:, k, :],
                                          lambda i, k: xs[:, i, k, :], k_wait=k_wait if (m, b) == (0, 0) else None)
                        if b == 0:
                            used("unit_used")
                    last.then_inc(S("up_done"), 1)
                    used("unit_used")

            def ffn_down(u, opening, closing):
                pe.wait_ge(S("hid_ready"), 2 * u + 2)
                for k in range(2):
                    w = unit(1)
                    for m in range(KT):
                        for i, (l, r) in enumerate(((0, 0), (0, 1), (1, 0))):
                            last = mm(pd[:, m // 2, (m % 2) * T:(m % 2 + 1) * T], w[l][:, 0, m * P:(m + 1) * P],
                                      hid[:, u % 2, r, k, :], opening and k == 0 and i == 0 and m % 2 == 0,
                                      closing and k == 1 and i == 2, True)
                        if closing and k == 1 and m % 2:
                            last.then_inc(S("down_done"), 1)
                    used("unit_used")

            for e in range(EXPERTS):
                ffn_up(e)
                if e == 0:
                    pe.wait_ge(S("combine"), 1)
                    for s in range(TT):
                        last = mm(pm[1][0:16, s * P:(s + 1) * P], combine[:, 16 * s:16 * s + 16], ident, True, True)
                    last.then_inc(S("combine_t"), 1)
                    pe.wait_ge(S("cmt_ready"), 1)
                    for i in range(EXPERTS):
                        if i >= 8 and i % 2 == 0:
                            pe.wait_ge(S("comb_out"), i // 2 - 3)
                        last = mm(pd[:, (i // 2) % 4, (i % 2) * T:(i % 2 + 1) * T],
                                  ident[0:16, i:i + 1].to_broadcast([16, P]), cmt[:, :], True, True)
                        if i % 2:
                            last.then_inc(S("comb_done"), 1)
                    pe.wait_ge(S("comb_out"), 8)
                else:
                    ffn_down(e - 1, e == 1, False)
            ffn_down(EXPERTS - 1, False, True)
            norm_sums(2, False)

            def values(dst, bias=None):
                n = at[0] - split0
                at[0] += 2
                assert n % NSPLIT + 2 <= NSPLIT
                pe.wait_ge(S("low_done"), n + 2)
                w = wsplit[:, n % NSPLIT:n % NSPLIT + 2, :, :]
                for t in range(TT):
                    cols = dst[:, t * T:(t + 1) * T]
                    for k in range(KT):
                        for i, (l, r) in enumerate(((0, 0), (1, 0), (0, 1))):
                            last = mm(cols, xs[:, l, k, t * P:(t + 1) * P], w[:, :, r, k * P:(k + 1) * P],
                                      k == 0 and i == 0, k == KT - 1 and i == 2 and bias is None)
                    if bias is not None:
                        last = mm(cols, ones[0:1, :], row("a_bv", bias, T), False, True)
                last.then_inc(S("v_done"), 1)
                used("two_used")

            def attn_project(q):
                layer, quad = q // 4, q % 4
                kind = KINDS[layer]
                first_wait = 8 * (1 + 2 * layer) if quad == 0 else None

                def job(e, i, tiles, first_wait=None):
                    if e >= 2:
                        pe.wait_ge(S("raw_out"), e - 1)
                    for m in range(tiles):
                        w = unit()
                        last = three_pass(pg[i][:, m * T:(m + 1) * T], lambda i, k: w[i][:, k, :],
                                          lambda i, k: xs[:, i, k, :], k_wait=first_wait)
                        first_wait = None
                        if m < tiles - 1:
                            used("unit_used")
                    last.then_inc(S("proj_done"), 1)
                    used("unit_used")

                if q >= 2:
                    pe.wait_ge(S("o_out"), q - 1 if q % 4 else q)
                for g in range(GROUPS[kind]):
                    e = 2 * (PROJ[q] + g)
                    if kind == 0:
                        job(e, 1, 1, first_wait)
                        if quad == 0:
                            if q:
                                pe.wait_ge(S("v_out"), VJOBS[q])
                            values(pm[1], (layer // 3) * T)
                    else:
                        if first_wait is not None:
                            for k in range(KT):
                                pe.wait_ge(S("x_ready"), first_wait + k + 1)
                            first_wait = None
                        pe.wait_ge(S("v_out"), VJOBS[q] + g)
                        values(pm[1])
                        if g:
                            attn_turned_pairs(kind, e - 1)
                        job(e, 1, 2)
                    job(e + 1, 0, 2)
                    attn_turned_pairs(kind, e)

            def attn_turned_pairs(kind, e):
                i = e % 2
                pe.wait_ge(S("raw_out"), e + 1)
                if e:
                    pe.wait_ge(S("rope_done"), e)
                for m in range(1 if kind == 0 and i == 0 else 2):
                    for half in range(2):
                        c = m * T + half * P
                        last = mm(pm[0][:, c:c + P], rot, raw[:, i, m, half * P:(half + 1) * P], True, True)
                last.then_inc(S("rot_done"), 1)

            def attn_outputs(q):
                pe.wait_ge(S("o_out"), q + 1)
                for i in range(4):
                    last = nc.tensor.transpose(
                        pd[:, 2, (i // 2) * T + (i % 2) * P:(i // 2) * T + (i % 2 + 1) * P],
                        osb[:, i % 2, 2 * (i // 2):2 * (i // 2) + 2, :].rearrange("p h d -> p (h d)"), ident)
                last.then_inc(S("ot_done"), 1)

            def attn_scores(q):
                kind = KINDS[q // 4]
                pe.wait_ge(S("rope_done"), 2 * PROJ[q + 1])
                for h in range(4):
                    for g in range(GROUPS[kind]):
                        u = 4 * PROJ[q] + h * GROUPS[kind] + g
                        if q % 4 and u - 4 * PROJ[q] == 2:
                            attn_outputs(q - 1)
                        if u >= 2:
                            pe.wait_ge(S("masked"), u - 1)
                        lo = HD * (h % 2)
                        kh = 0 if kind == 0 else h // 2
                        mm(pd[:, u % 2, 0:P], qr[lo:lo + HD, g, h // 2, 0:P], kr[lo:lo + HD, g, kh, 0:P], True, True)
                        mm(pd[:, u % 2, P:P + T], qr[lo:lo + HD, g, h // 2, P:T], kr[lo:lo + HD, g, kh, :],
                           True, True).then_inc(S("scored"), 1)

            def attn_values(q):
                kind = KINDS[q // 4]
                G = GROUPS[kind]

                def weigh(j):
                    h, g = j // G, j % G
                    u = 4 * PROJ[q] + j
                    pe.wait_ge(S("pt_out"), u + 1)
                    col = 0 if kind == 0 else h * HD
                    v = vt[:, 0, 0, :, (q % 4) * HD:(q % 4 + 1) * HD] if kind == 0 else vt[:, q % 2, g, :, col:col + HD]
                    mm(pg[0][:, h * HD:(h + 1) * HD], pt[:, u % 2, 0:P], v[:, 0, :], g == 0, g == G - 1)
                    mm(pg[1][:, h * HD:(h + 1) * HD], pt[:, u % 2, P:2 * P], v[:, 0, :], g == 0, False)
                    return mm(pg[1][:, h * HD:(h + 1) * HD], pt[:, u % 2, 2 * P:3 * P], v[:, 1, :], False, g == G - 1)

                pe.wait_ge(S("raw_out"), 2 * PROJ[q + 1 if q % 4 == 3 else q + 2])
                if q:
                    pe.wait_ge(S("otl_out"), q)
                for j in range(4 * G):
                    h, g = j // G, j % G
                    u = 4 * PROJ[q] + j
                    pe.wait_ge(S("exped"), 4 * q + h + 1)
                    if u >= 2:
                        pe.wait_ge(S("pt_out"), u - 1)
                    nc.tensor.transpose(pd[:, 2 + u % 2, 0:P], s0[:, h, g * P:(g + 1) * P], ident)
                    nc.tensor.transpose(pd[:, 2 + u % 2, P:2 * P], s1[:, h, g * T:g * T + P], ident)
                    nc.tensor.transpose(pd[:, 2 + u % 2, 2 * P:3 * P], s1[:, h, g * T + P:(g + 1) * T], ident
                                        ).then_inc(S("pt_done"), 1)
                    if j:
                        weigh(j - 1)
                    if j == 1 and q % 4 < 3:
                        attn_turned_pairs(kind, 2 * PROJ[q + 2] - 1)
                weigh(4 * G - 1).then_inc(S("o_done"), 1)
                if q % 4 == 3:
                    attn_outputs(q)

            for layer, kind in enumerate(KINDS):
                q0 = 4 * layer
                attn_project(q0)
                attn_turned_pairs(kind, 2 * PROJ[q0 + 1] - 1)
                for q in range(q0, q0 + 4):
                    attn_scores(q)
                    if q < q0 + 3:
                        attn_project(q + 1)
                    attn_values(q)
                pe.wait_ge(S("otl_out"), q0 + 4)
                for j in range(4):
                    if j >= 2:
                        pe.wait_ge(S("res_ready"), 8 * (2 + 2 * layer) + 2 * (j - 1))
                    for i in range(2):
                        w = unit()
                        last = three_pass(pg[j % 2][:, i * T:(i + 1) * T], lambda i, k: w[i][:, k, :],
                                          lambda i, k: (oth, otl)[i][:, k, :])
                        if i == 0:
                            used("unit_used")
                    last.then_inc(S("square_done"), 1)
                    used("unit_used")
                norm_sums(3 + 2 * layer, True)
                u0 = EXPERTS + NFF * layer
                for i in range(NFF):
                    ffn_up(u0 + i, 8 * (2 + 2 * layer) if i == 0 else None)
                    if i:
                        ffn_down(u0 + i - 1, i == 1, False)
                ffn_down(u0 + NFF - 1, False, True)
                norm_sums(4 + 2 * layer, True)

        @block.scalar
        def _(act):
            steps = [0]

            def then(ins):
                steps[0] += 1
                ins.then_inc(S("scalar_step"), 1)
                act.wait_ge(S("scalar_step"), steps[0])

            loads = [(x[:, :, :], a["x"].rearrange("(k p) t -> p k t", p=P)),
                     (cx[:, :, :], a["ctx"].rearrange("(k p) t -> p k t", p=P)),
                     (consts[:, :], a["consts"]), (vecs[:, :], a["vecs"]), (rows[:, :], a["rows"]),
                     (hyf[:, :], a["hyf"]), (ar[0:33, 1280:1344], a["hy_w1"]), (hyw[:, 64:128], a["hy_w2"]),
                     (feat, a["feat"]), (wg16[:, :, :], a["w_gates"]), (wr20[:, :, :], a["w_route"]),
                     (sinks[:, :], a["sinks"].partition_broadcast(P)),
                     (posi, a["positions"].partition_broadcast(P))]
            assert len(loads) == NLOADS
            for dst, src in loads:
                act.dma_start(dst, src).then_inc(S("loaded"), 16)
            at = [split0]

            def split_to(n):
                while at[0] <= min(n, len(units) - 1):
                    s = at[0]
                    c = s // CHUNK
                    await_chunk(act, c)
                    if s >= split0 + NSPLIT:
                        act.wait_ge(S("unit_used"), s - split0 - NSPLIT + 1)
                    nc.scalar.copy(wsplit[:, (s - split0) % NSPLIT, 0, :], ring[:, s % NRAW, :]
                                   ).then_inc(S("high_done"), 1)
                    at[0] += 1

            act.wait_ge(S("loaded"), 16 * NLOADS)
            act.wait_ge(S("angles"), 1)
            nc.scalar.activation(ropes[:, :, :], ropes[:, :, :], ACT.Sin).then_inc(S("rope_sin"), 1)
            act.wait_ge(S("hy_arg"), 1)
            nc.scalar.activation(hyh[:, 3, :], hyh[:, 2, :], ACT.Sin).then_inc(S("hy_sin"), 1)
            act.wait_ge(S("hy_arg"), 2)
            nc.scalar.activation(hyh2[:, :], hyh[:, 2, :], ACT.Sin).then_inc(S("hy_sin"), 1)
            nc.scalar.activation(cs[:, :], vecs[:, VOFF["c"]:VOFF["c"] + 16], ACT.Silu).then_inc(S("c_silu"), 1)

            nc.scalar.activation(sq2[:, :, 0:T], x[:, :, :], ACT.Square).then_inc(S("nrm_sq"), 1)
            nc.scalar.activation(sq2[:, :, T:2 * T], cx[:, :, :], ACT.Square).then_inc(S("nrm_sq"), 1)
            for j in range(12):
                act.wait_ge(S("mod_done"), j + 1)
                nc.scalar.copy(mod_row[:, j * 512:(j + 1) * 512], pg[j % 2][0:2, :]).then_inc(S("mod_row"), 1)

            def square_root(n, width):
                act.wait_ge(S("nrm_eps"), n + 1)
                nc.scalar.activation(nrm[:, 1, 0:width], nrm[:, 0, 0:width], ACT.Sqrt).then_inc(S("nrm_root"), 1)

            square_root(0, 2 * T)
            for half in range(2):
                act.wait_ge(S("nrm_scaled"), half + 1)
                for k in range(KT):
                    h = hc[:, k, half * T:(half + 1) * T]
                    nc.scalar.activation(h, h, ACT.Identity, bias=modv[:, k, half:half + 1],
                                         scale=gain[:, k, half:half + 1]).then_inc(S("h_ready"), 1)

            act.wait_ge(S("pads_zero"), 1)
            for j in range(32):
                act.wait_ge(S("in_done"), j + 1)
                p = pg[j % 2]
                if j < 4:
                    nc.scalar.copy(vx[:, j, :, 0:P], p[:, :].rearrange("p (h v) -> p h v", v=P)
                                   ).then_inc(S("in_out"), 1)
                elif j < 8:
                    i = j - 4
                    if i >= 2:
                        act.wait_ge(S("conv_out"), 1)
                    nc.scalar.activation(kpad[:, i % 2, 1:T + 1], p[:, T:2 * T], ACT.Identity, bias=vec("b_in", i))
                    nc.scalar.activation(zring[:, i, 1:5, 1:65], p[:, 0:T].rearrange("p (r c) -> p r c", c=64),
                                         ACT.Identity, bias=vec("b_in", i)).then_inc(S("in_out"), 1)
                    if i == 3:
                        act.wait_ge(S("gates_raw"), 1)
                        for r in range(4):
                            kind, lo = ((0, 0), (1, 0), (2, 4), (3, 4))[r]
                            last = nc.scalar.copy(zp[:, kind, :, lo:lo + 4],
                                                  pm[0][:, 0:64].rearrange("p (s c) -> p s c", c=16)[:, :, 4 * r:4 * r + 4])
                        last.then_inc(S("zp_ready"), 1)
                else:
                    b = 8 + 2 * (j - 8)
                    for i in range(2):
                        src, bias = p[:, i * T:(i + 1) * T], vec("b_in", b - 4 + i)
                        if b < 24:
                            c = b - 4 + i
                            if c >= 8 and i == 0:
                                act.wait_ge(S("conv_out"), c // 2 - 3)
                            last = nc.scalar.activation(zring[:, c % 8, 1:5, 1:65],
                                                        src.rearrange("p (r c) -> p r c", c=64),
                                                        ACT.Identity, bias=bias)
                        elif b < 28:
                            last = nc.scalar.activation(zfn[:, b - 24 + i, :], src, ACT.Identity, bias=bias)
                        elif b < 32:
                            last = nc.scalar.activation(osig[:, b - 28 + i, :], src, ACT.Sigmoid, bias=bias)
                        else:
                            last = nc.scalar.activation(g_sig[:, b - 32 + i, :], src, ACT.Sigmoid, bias=bias)
                    last.then_inc(S("in_out"), 1)

            act.wait_ge(S("conv_out"), 10)
            nc.scalar.activation(qf, qf, ACT.Silu)
            nc.scalar.activation(kf, kf, ACT.Silu)
            nc.scalar.activation(kc, kc, ACT.Silu).then_inc(S("qk_silu"), 1)
            act.wait_ge(S("forget_min"), 1)
            then(nc.scalar.activation(rr[:, 0, :], pm[0][0:8, :], ACT.Abs))
            then(nc.scalar.activation(rr[:, 0, :], rr[:, 0, :], ACT.Exp, scale=-1.0))
            nc.scalar.activation(rr[:, 0, :], rr[:, 0, :], ACT.Ln, bias=1.0).then_inc(S("softplus"), 1)
            act.wait_ge(S("gate_cols"), 1)
            nc.scalar.copy(ct[:, :, :], pm[1][:, 0:64].rearrange("p (n c) -> p n c", c=8)).then_inc(S("ct_ready"), 1)
            act.wait_ge(S("gate_back"), 1)
            nc.scalar.copy(cb[:, :, :], pm[0][:, 0:32].rearrange("p (n c) -> p n c", c=4)).then_inc(S("cb_ready"), 1)
            act.wait_ge(S("back_rows"), 1)
            nc.scalar.copy(rb[:, :], pm[1][0:4, 0:T]).then_inc(S("rb_ready"), 1)
            act.wait_ge(S("rb_ready"), 1)
            for t in range(2):
                nc.scalar.activation(ecol[:, 0, t, :], ct[:, 6 + t, 0:4], ACT.Exp)
                last = nc.scalar.activation(ecol[:, 1, t, :], cb[:, 7 - t, :], ACT.Exp)
            last.then_inc(S("floors"), 1)
            for h in range(MLH):
                act.wait_ge(S("qk_done"), h + 1)
                if h:
                    act.wait_ge(S("smat_done"), 8 * h)
                nc.scalar.activation(qks, pd[:, 0:2, :].rearrange("p b (s t) -> p (b s) t", t=T), ACT.Copy,
                                     scale=P ** -0.5).then_inc(S("qk_out"), 1)
                nc.scalar.copy(negm, pm[0][:, :]).then_inc(S("negm_out"), 1)
                act.wait_ge(S("negm_out"), h + 1)
                for d in range(2):
                    for i in range(4):
                        e = 8 * h + 4 * d + i
                        if e >= 2:
                            act.wait_ge(S("smat_done"), e - 1)
                        if i < 2:
                            src = negm[:, d * T:(d + 1) * T]
                        else:
                            act.wait_ge(S("wtmp_done"), 4 * h + 2 * d + i - 1)
                            src = wtmp[:, i % 2, :]
                        g = ct[:, i, h:h + 1] if d == 0 else cb[:, (1, 0, 3, 2)[i], h:h + 1]
                        nc.scalar.activation(wexp[:, e % 2, :], src, ACT.Exp, bias=g).then_inc(S("wexp_done"), 1)
            act.wait_ge(S("ml_evac"), 2 * MLH)
            for t in range(2):
                for h in range(MLH):
                    last = nc.scalar.activation(wtmp[:, 0, 0:P], hml[:, t, h, :], ACT.Square,
                                                accum_out=ml_ss[:, 4 * t + h:4 * t + h + 1])
                    if (t, h) != (1, MLH - 1):
                        then(last)
            last.then_inc(S("ml_squares"), 1)
            act.wait_ge(S("ml_eps"), 1)
            then(nc.scalar.activation(ml_y, ml_ve, ACT.Ln))
            nc.scalar.activation(ml_y, ml_y, ACT.Exp, scale=-0.5).then_inc(S("ml_log"), 1)

            for g in range(BT):
                act.wait_ge(S("fn_first"), g + 1)
                if g >= 2:
                    act.wait_ge(S("fn_second"), g - 1)
                nc.scalar.copy(fnp[:, g % 2, :], pg[g % 2][:, :]).then_inc(S("fn_p"), 1)

            for o in range(2):
                act.wait_ge(S("decay_landed"), 32 * (o + 1))
                then(nc.scalar.activation(hdec, hdec, ACT.Abs))
                for t in range(TT):
                    tc = consts[:, COFF["tcol"] + t:COFF["tcol"] + t + 1]
                    nc.scalar.activation(hdec[:, t, 0:DB], hdec[:, t, 0:DB], ACT.Exp, scale=tc)
                    last = nc.scalar.activation(hdec[:, t, DB:2 * DB], hdec[:, t, DB:2 * DB], ACT.Exp, scale=tc,
                                                bias=consts[:, COFF["drop0"] + t:COFF["drop0"] + t + 1])
                last.then_inc(S("hy_decays"), 1)
                act.wait_ge(S("hy_tapped"), o + 1)
                nc.scalar.activation(hdec.rearrange("p s n -> p (s n)"), hk.rearrange("p s d c -> p (s d c)"),
                                     ACT.Square).then_inc(S("hy_tapsq"), 1)
                for m in range(5):
                    act.wait_ge(S("hy_spec"), 5 * o + m + 1)
                    if m == 0:
                        act.wait_ge(S("hy_eps"), o + 1)
                        then(nc.scalar.activation(hy_rk[:, 4 * o:4 * o + 4], hy_ve[:, 4 * o:4 * o + 4], ACT.Ln))
                        nc.scalar.activation(hy_rk[:, 4 * o:4 * o + 4], hy_rk[:, 4 * o:4 * o + 4], ACT.Exp,
                                             scale=-0.5).then_inc(S("hy_log"), 1)
                    nc.scalar.copy(kfr[:, m, :], pg[m % 2][:, :]).then_inc(S("hy_specout"), 1)

            def squares(n, src, dst, wait):
                for i in range(4):
                    act.wait_ge(*wait(i))
                    nc.scalar.activation(dst[:, 2 * i:2 * i + 2, :], src[:, 2 * i:2 * i + 2, :],
                                         ACT.Square).then_inc(S("nrm_sq"), 1)
                square_root(n, T)

            def normed(n, dst, biases=None, final=False):
                for k in range(KT):
                    act.wait_ge(S("x_scaled"), 8 * (n - 1) + k + 1)
                    if biases is None:
                        nc.scalar.copy(dst[:, k, :], sq1[:, k, :]).then_inc(S("x_full"), 1)
                        nc.scalar.copy(xs[:, 0, k, :], sq1[:, k, :]).then_inc(S("x_high"), 1)
                        continue
                    nc.scalar.activation(dst[:, k, :], sq1[:, k, :], ACT.Identity, bias=biases(k)
                                         ).then_inc(S("x_full"), 1)
                    if not final:
                        nc.scalar.activation(xs[:, 0, k, :], sq1[:, k, :], ACT.Identity, bias=biases(k)
                                             ).then_inc(S("x_high"), 1)

            squares(1, x, sq1, lambda i: (S("res_ready"), 2 * i + 2))
            split_to(split0 + NSPLIT - 1)
            normed(1, h1, lambda k: modv[:, 24 + k, 0:1])
            act.wait_ge(S("group_diff"), 1)
            nc.scalar.activation(route[:, 40:48], route[:, 40:48], ACT.Exp).then_inc(S("group_exp"), 1)
            act.wait_ge(S("pair_diff"), 1)
            nc.scalar.activation(route[:, 100:102], route[:, 100:102], ACT.Exp).then_inc(S("pair_exp"), 1)
            split_to(split0 + 3)
            act.wait_ge(S("combine_t"), 1)
            nc.scalar.copy(cmt[:, :], pm[1][0:16, 0:T]).then_inc(S("cmt_ready"), 1)
            for i in range(8):
                act.wait_ge(S("comb_done"), i + 1)
                nc.scalar.copy(comb[:, 2 * i:2 * i + 2, :], pd[:, i % 4, :].rearrange("p (e t) -> p e t", t=T)
                               ).then_inc(S("comb_out"), 1)

            def ffn_act(u, s0, first, final):
                e = s0 + (0 if first else 6 * (u - UFIRST[u]) - 2)
                for m in range(2):
                    split_to(e + 2 * m + 3)
                    act.wait_ge(S("up_done"), 2 * u + m + 1)
                    if u:
                        act.wait_ge(S("hid_raw"), 2 * (u - 1) + m + 1)
                    nc.scalar.activation(silu_g[:, m, :], pg[m][:, 0:T], ACT.Silu).then_inc(S("silu_done"), 1)
                    act.wait_ge(S("hid_raw"), 2 * u + m + 1)
                    nc.scalar.copy(hid[:, u % 2, 0, m, :], htmp[:, m, :]).then_inc(S("hid_high"), 1)
                if final:
                    split_to(s0 + 6 * (u - UFIRST[u] + 1) + 1)

            for e in range(EXPERTS):
                ffn_act(e, split0, e == 0, e == EXPERTS - 1)

            squares(2, x, sq1, lambda i: (S("res_ready"), 8 + (2 * i + 2 if i < 2 else 8)))
            normed(2, x)

            def attn_gather(q):
                layer, kind = q // 4, KINDS[q // 4]
                end = QUNIT[q] - 1

                def take_values(g):
                    act.wait_ge(S("v_done"), VJOBS[q] + g + 1)
                    nc.scalar.copy(vt[:, 0 if kind == 0 else q % 2, g, :, :],
                                   pm[1][:, :].rearrange("p (s c) -> p s c", c=T)).then_inc(S("v_out"), 1)

                for g in range(GROUPS[kind]):
                    if kind:
                        end += 2
                        split_to(end + 2)
                        take_values(g)
                    for i in range(2):
                        e = 2 * (PROJ[q] + g) + i
                        end += 1 if kind == 0 and i == 0 else 2
                        split_to(end + (1 if kind == 0 and i == 0 and q % 4 == 0 else 2))
                        act.wait_ge(S("proj_done"), e + 1)
                        if e >= 2:
                            act.wait_ge(S("rope_done"), e - 1)
                        if kind == 0:
                            if i:
                                for m in range(2):
                                    last = nc.scalar.activation(raw[:, 1, m, :], pg[0][:, m * T:(m + 1) * T], ACT.Identity,
                                                                bias=vec("a_bq", 8 * (layer // 3) + 2 * (q % 4) + m))
                            else:
                                last = nc.scalar.activation(raw[:, 0, 0, :], pg[1][:, 0:T], ACT.Identity,
                                                            bias=vec("a_bk", 4 * (layer // 3) + q % 4))
                        else:
                            last = nc.scalar.copy(raw[:, i, :, :], pg[1 - i][:, :].rearrange("p (m t) -> p m t", t=T))
                        last.then_inc(S("raw_out"), 1)
                        if kind == 0 and i == 0 and q % 4 == 0:
                            end += 2
                            split_to(end + 1)
                            take_values(0)
                split_to(end + 3)

            def attn_exp(q):
                kind = KINDS[q // 4]
                sink = 1 if kind == 0 else 0
                w = GROUPS[kind] * P
                for h in range(4):
                    act.wait_ge(S("smax"), 4 * q + h + 1)
                    nc.scalar.activation(s0[:, h, 0:w + sink], s0[:, h, 0:w + sink], ACT.Exp,
                                         bias=smx[:, 0, 0, h:h + 1], accum_out=smx[:, 1, 0, h:h + 1])
                    nc.scalar.activation(s1[:, h, 0:2 * w + sink], s1[:, h, 0:2 * w + sink], ACT.Exp,
                                         bias=smx[:, 0, 1, h:h + 1], accum_out=smx[:, 1, 1, h:h + 1]
                                         ).then_inc(S("exped"), 1)

            def attn_turn(q):
                G = GROUPS[KINDS[q // 4]]
                for j in range(4 * G):
                    u = 4 * PROJ[q] + j
                    act.wait_ge(S("pt_done"), u + 1)
                    nc.scalar.copy(pt[:, u % 2, :], pd[:, 2 + u % 2, 0:3 * P]).then_inc(S("pt_out"), 1)
                act.wait_ge(S("ot_done"), q + 1)
                nc.scalar.copy(oth[:, 2 * (q % 4):2 * (q % 4) + 2, :],
                               pd[:, 2, :].rearrange("p (k t) -> p k t", t=T)).then_inc(S("oth_out"), 1)

            for layer in range(LAYERS):
                q0 = 4 * layer
                attn_gather(q0)
                for q in range(q0, q0 + 4):
                    attn_exp(q)
                    if q < q0 + 3:
                        attn_gather(q + 1)
                    attn_turn(q)
                if KINDS[layer] == 0:
                    for k in range(KT):
                        last = nc.scalar.activation(x[:, k, :], x[:, k, :], ACT.Identity, scale=ALPHA,
                                                    bias=vec("a_bo", 8 * (layer // 3) + k))
                    last.then_inc(S("x_biased"), 1)
                last = first[("wo", layer)] + 7
                split_to(last + 2)
                for i in range(2):
                    n = 3 + 2 * layer + i
                    squares(n, x, sq1, lambda i: (S("ln_centered"), 4 * (n - 3) + i + 1))
                    normed(n, x, lambda k: vec("ln_b", 8 * (n - 3) + k), n == 2 + 2 * LAYERS)
                    if i == 0:
                        for j in range(NFF):
                            ffn_act(EXPERTS + NFF * layer + j, last + 1, j == 0, j == NFF - 1)

        @block.vector
        def _(dve):
            V = nc.vector
            steps = [0]

            def then(ins):
                steps[0] += 1
                ins.then_inc(S("vector_step"), 1)
                dve.wait_ge(S("vector_step"), steps[0])

            def wrap(arg, turns):
                then(V.tensor_scalar(turns, arg, 1.0 / TWO_PI, MAGIC, ALU.mult, ALU.add))
                then(V.tensor_scalar(turns, turns, MAGIC, None, ALU.subtract))
                for part in TWO_PI_PARTS:
                    then(V.scalar_tensor_tensor(arg, turns, -part, arg, ALU.mult, ALU.add))
                then(V.tensor_scalar(arg, arg, -PI32, PI32, ALU.max, ALU.min))

            def newton(y, v, t):
                then(V.tensor_tensor(t, y, y, ALU.mult))
                then(V.tensor_tensor(t, t, v, ALU.mult))
                then(V.tensor_scalar(t, t, -0.5, 1.5, ALU.mult, ALU.add))
                then(V.tensor_tensor(y, y, t, ALU.mult))

            at = [split0]

            def split_to(n):
                while at[0] <= min(n, len(units) - 1):
                    s = at[0]
                    dve.wait_ge(S("high_done"), s - split0 + 1)
                    w = wsplit[:, (s - split0) % NSPLIT, :, :]
                    V.tensor_tensor(w[:, 1, :], ring[:, s % NRAW, :], w[:, 0, :].bitcast(F32), ALU.subtract
                                    ).then_inc(S("low_done"), 1)
                    at[0] += 1

            dve.wait_ge(S("loaded"), 16 * NLOADS)
            then(V.tensor_copy(ropes[:, 0, :], posi[:, :]))
            then(V.tensor_scalar(ropes[:, 0, :], ropes[:, 0, :], consts[:, COFF["freq"]:COFF["freq"] + 1], None, ALU.mult))
            wrap(ropes[:, 0, :], ropes[:, 1, :])
            then(V.tensor_copy(ropes[:, 1, :], ropes[:, 0, :]))
            V.tensor_scalar(ropes[:, 0, :], ropes[:, 0, :], 0.5, None, ALU.mult).then_inc(S("angles"), 1)
            for i in range(2):
                dve.wait_ge(S("hy_net"), i + 1)
                if i:
                    dve.wait_ge(S("hy_sin"), 1)
                then(V.tensor_scalar(hyh[:, 0, :], pg[i][0:64, 0:T], hyf[:, i:i + 1], hyf[:, 2:3], ALU.add, ALU.mult))
                wrap(hyh[:, 0, :], hyh[:, 1, :])
                V.tensor_copy(hyh[:, 2, :], hyh[:, 0, :]).then_inc(S("hy_arg"), 1)
            dve.wait_ge(S("rope_sin"), 1)
            then(V.tensor_tensor(ropes[:, 0, :], ropes[:, 0, :], ropes[:, 0, :], ALU.mult))
            then(V.tensor_scalar(ropes[:, 0, :], ropes[:, 0, :], -2.0, 1.0, ALU.mult, ALU.add))

            dve.wait_ge(S("mod_raw"), 1)
            adab = vecs[:, VOFF["ada_b"]:VOFF["ada_b"] + 48]
            then(V.tensor_tensor(modv[:, :, :], pm[0][:, 0:96].rearrange("p (f j) -> p f j", j=2),
                                 adab.unsqueeze(2).to_broadcast([P, 48, 2]), ALU.add))
            for j, (part, w) in enumerate(((8, "norm1_w"), (8, "norm1_w"), (32, "norm2_w"))):
                V.scalar_tensor_tensor(gain[:, :, j], modv[:, part:part + 8, j % 2], 1.0,
                                       vecs[:, VOFF[w]:VOFF[w] + 8], ALU.add, ALU.mult)
            then(V.memset(small[:, 255:256], 0.0))

            def root(n, width, eps):
                dve.wait_ge(S("nrm_var"), n + 1)
                V.tensor_scalar(nrm[:, 0, 0:width], pm[1][:, 0:width], eps, None, ALU.add).then_inc(S("nrm_eps"), 1)
                dve.wait_ge(S("nrm_root"), n + 1)
                y, v, t = (nrm[:, i, 0:width] for i in (1, 0, 2))
                then(V.reciprocal(y, y))
                then(V.scalar_tensor_tensor(t, y, -0.5, y, ALU.mult, ALU.mult))
                then(V.tensor_tensor(t, t, v, ALU.mult))
                then(V.scalar_tensor_tensor(y, t, 1.5, y, ALU.add, ALU.mult))

            def scale_by_root(dst, src, lo=0, tiles=KT):
                return V.tensor_tensor(dst, src, nrm[:, 1, lo:lo + T].unsqueeze(1).to_broadcast([P, tiles, T]),
                                       ALU.mult)

            root(0, 2 * T, EPS_RMS)
            scale_by_root(hc[:, :, 0:T], x[:, :, :]).then_inc(S("nrm_scaled"), 1)
            scale_by_root(hc[:, :, T:2 * T], cx[:, :, :], T).then_inc(S("nrm_scaled"), 1)

            for pair in range(10):
                tiles = [2 * pair, 2 * pair + 1]
                if pair < 2:
                    dve.wait_ge(S("in_out"), 4 + 2 * pair + 2)
                else:
                    dve.wait_ge(S("in_out"), 8 + pair - 1)

                def conv_taps(c):
                    if c < 8:
                        ch = c + 4 if c < 4 else c - 4
                        return [vec("ml_conv_w", 9 * ch + i) for i in range(9)], vec("ml_conv_b", ch)
                    return [vec("hy_conv_w", 9 * (c - 8) + i) for i in range(9)], vec("hy_conv_b", c - 8)

                dsts = [(kf[:, c] if c < 4 else qf[:, c - 4] if c < 8 else hyc[:, c - 8]) for c in tiles]
                for i in range(9):
                    for c, dst in zip(tiles, dsts):
                        w, b = conv_taps(c)
                        src = zring[:, c % 8, i // 3:i // 3 + 4, i % 3:i % 3 + 64]
                        d = dst.rearrange("p (r c) -> p r c", c=64)
                        if i == 0:
                            last = V.tensor_scalar(d, src, w[0], b, ALU.mult, ALU.add)
                        else:
                            last = V.scalar_tensor_tensor(d, src, w[i], d, ALU.mult, ALU.add)
                    if i < 8 or pair < 2:
                        then(last)
                if pair < 2:
                    for i in range(3):
                        for c in tiles:
                            w, b = conv_taps(c)
                            src = kpad[:, c % 2, i:i + T]
                            if i == 0:
                                last = V.tensor_scalar(kc[:, c], src, w[3], b, ALU.mult, ALU.add)
                            else:
                                last = V.scalar_tensor_tensor(kc[:, c], src, w[3 + i], kc[:, c], ALU.mult, ALU.add)
                        if i < 2:
                            then(last)
                last.then_inc(S("conv_out"), 1)

            dve.wait_ge(S("gate_rows"), 1)
            dve.wait_ge(S("conv_out"), 10)
            V.tensor_scalar(rr[:, 1, :], pm[0][0:8, :], 0.0, None, ALU.min).then_inc(S("forget_min"), 1)
            dve.wait_ge(S("softplus"), 1)
            then(V.tensor_tensor(rr[:, 1, :], rr[:, 1, :], rr[:, 0, :], ALU.subtract))
            one = ones[0:8, 0:1].to_broadcast([8, 512])
            then(V.tensor_tensor_scan(rr[:, 2, :], one, rr[:, 1, :], 0.0, ALU.mult, ALU.add))
            then(V.tensor_tensor(rr[:, 3, :], pm[1][0:8, :], rr[:, 2, :], ALU.subtract))
            then(V.tensor_tensor_scan(rr[:, 4, :], one, rr[:, 3, :], 0.0, ALU.mult, ALU.max))
            then(V.tensor_scalar(rr[:, 5, :], rr[:, 4, :], -1.0, None, ALU.mult))
            V.tensor_tensor(rr[:, 6, :], rr[:, 5, :], rr[:, 2, :], ALU.subtract).then_inc(S("rows_done"), 1)
            dve.wait_ge(S("cx_tables"), 16)
            dve.wait_ge(S("floors"), 1)
            for h in range(MLH):
                for d in range(2):
                    dve.wait_ge(S("negm_out"), h + 1)
                    for i in range(2):
                        V.tensor_tensor(wtmp[:, i, :], negm[:, d * T:(d + 1) * T], mlmask[:, d, i, :], ALU.add
                                        ).then_inc(S("wtmp_done"), 1)
                    dve.wait_ge(S("qk_out"), h + 1)
                    for i in range(4):
                        e = 8 * h + 4 * d + i
                        dve.wait_ge(S("wexp_done"), e + 1)
                        if e >= 2:
                            dve.wait_ge(S("smat_used"), e - 1)
                        V.tensor_tensor(smat[:, i % 2, :], qks[:, (2, 3, 0, 1)[i], :], wexp[:, e % 2, :], ALU.mult
                                        ).then_inc(S("smat_done"), 1)
                    dve.wait_ge(S("smat_used"), 8 * h + 4 * d + 4)
                    sums = [(pd[:, 2 + t, :], pg[t][:, :])[d] for t in range(2)]
                    for t in range(2):
                        last = V.tensor_scalar(ml_den[:, t:t + 1], sums[t][:, P:P + 1], -1.0, None, ALU.mult)
                    then(last)
                    for t in range(2):
                        last = V.tensor_tensor(ml_den[:, t:t + 1], ml_den[:, t:t + 1], sums[t][:, P:P + 1], ALU.max)
                    then(last)
                    then(V.tensor_tensor(ml_den, ml_den, ecol[:, d, :, h], ALU.max))
                    then(V.reciprocal(ml_rl, ml_den))
                    for t in range(2):
                        src = sums[t][:, 0:P]
                        if d == 0:
                            last = V.tensor_scalar(hml[:, t, h, :], src, ml_rl[:, t:t + 1], None, ALU.mult)
                        else:
                            last = V.scalar_tensor_tensor(hml[:, t, h, :], src, ml_rl[:, t:t + 1], hml[:, t, h, :],
                                                          ALU.mult, ALU.add)
                    last.then_inc(S("ml_evac"), 1)
                    dve.wait_ge(S("ml_evac"), 2 * h + d + 1)
            dve.wait_ge(S("ml_squares"), 1)
            V.tensor_scalar(ml_ve, ml_ss, 1.0 / P, EPS_RMS, ALU.mult, ALU.add).then_inc(S("ml_eps"), 1)
            dve.wait_ge(S("ml_log"), 1)
            newton(ml_y, ml_ve, ml_t)
            hflat = hml.rearrange("p t h v -> p (t h) v")
            V.tensor_tensor(hflat, hflat, ml_y.unsqueeze(2).to_broadcast([P, 8, P]), ALU.mult
                            ).then_inc(S("hml_scaled"), 1)
            dve.wait_ge(S("hml_read"), 1)
            for h in range(MLH):
                last = V.scalar_tensor_tensor(osig[:, h, :], pd[:, h // 2, (h % 2) * T:(h % 2 + 1) * T],
                                              vec("ml_norm_w", h), osig[:, h, :], ALU.mult, ALU.mult)
            last.then_inc(S("y_ml"), 1)

            for g in range(BT):
                dve.wait_ge(S("fn_second"), g + 1)
                V.tensor_copy(zfn[:, g, :], pm[g % 2][:, 0:T]).then_inc(S("fn_out"), 1)

            for o in range(2):
                dve.wait_ge(S("hy_taps"), o + 1)
                dve.wait_ge(S("hy_decays"), o + 1)
                for t in range(TT):
                    last = V.tensor_tensor(hk[:, t, :, :], pd[:, 2 * t:2 * t + 2, :],
                                           hdec[:, t, :].rearrange("p (d c) -> p d c", d=2), ALU.mult)
                last.then_inc(S("hy_tapped"), 1)
                dve.wait_ge(S("hy_tapsq"), o + 1)
                for t in range(TT):
                    V.tensor_tensor(ptmp[:, t, :], hk[:, t, 0, :], hk[:, t, 1, :], ALU.add)
                    last = V.tensor_tensor(hk[:, t, 1, :], hk[:, t, 0, :], hk[:, t, 1, :], ALU.subtract)
                then(last)
                V.tensor_copy(hk[:, :, 0, :], ptmp).then_inc(S("hy_sides"), 1)
                dve.wait_ge(S("hy_energy"), o + 1)
                sl = slice(4 * o, 4 * o + 4)
                V.tensor_scalar(hy_ve[:, sl], pm[0][:, sl], EPS_RMS, None, ALU.add).then_inc(S("hy_eps"), 1)
                dve.wait_ge(S("hy_turned"), o + 1)
                V.tensor_copy(utok, pd[:, 0:2, :]).then_inc(S("hy_utok"), 1)
                dve.wait_ge(S("hy_fwd"), o + 1)
                dve.wait_ge(S("hy_specout"), 5 * o + 5)
                dve.wait_ge(S("hy_sides"), o + 1)
                for m, (p0, k0, p1, k1, op) in enumerate(((0, 0, 2, 2, ALU.subtract), (1, 1, 3, 3, ALU.subtract),
                                                          (0, 2, 2, 4, ALU.add), (1, 3, 3, 1, ALU.add))):
                    V.tensor_tensor(yfr[:, m, :], pd[:, p0, :], kfr[:, k0, :], ALU.mult)
                    then(V.tensor_tensor(ptmp[:, m % 2, :], pd[:, p1, :], kfr[:, k1, :], ALU.mult))
                    last = V.tensor_tensor(yfr[:, m, :], yfr[:, m, :], ptmp[:, m % 2, :], op)
                last.then_inc(S("hy_prod"), 1)
                dve.wait_ge(S("hy_log"), o + 1)
                newton(hy_rk[:, sl], hy_ve[:, sl], hy_t[:, sl])
                for c in range(BT):
                    u, g = hyc[:, 4 * o + c, :], hyc[:, 4 * o + 4 + c, :]
                    then(V.tensor_scalar(u, u, vec("hy_skip", 4 * o + c), None, ALU.mult))
                    if c == 0:
                        dve.wait_ge(S("hy_back"), o + 1)
                    then(V.scalar_tensor_tensor(u, pg[c // 2][:, (c % 2) * T:(c % 2 + 1) * T],
                                                hy_rk[:, 4 * o + c:4 * o + c + 1], u, ALU.mult, ALU.add))
                    last = V.tensor_tensor(g, g, u, ALU.mult)
                last.then_inc(S("hy_z"), 1)

            for m in range(KT):
                dve.wait_ge(S("branched"), m + 1)
                p = pd[:, 2 * (m % 2):2 * (m % 2) + 2, :]
                V.tensor_tensor(mix[:, m, :], p[:, 0, 0:T], g_sig[:, m, :], ALU.mult)
                if m:
                    dve.wait_ge(S("mixed"), m)
                V.tensor_tensor(mtmp[:, 0, :], p[:, 0, T:2 * T], g_sig[:, 8 + m, :], ALU.mult)
                then(V.tensor_tensor(mtmp[:, 1, :], p[:, 1, 0:T], g_sig[:, 16 + m, :], ALU.mult))
                then(V.tensor_tensor(mix[:, m, :], mix[:, m, :], mtmp[:, 0, :], ALU.add))
                V.tensor_tensor(mix[:, m, :], mix[:, m, :], mtmp[:, 1, :], ALU.add).then_inc(S("mixed"), 1)

            def residual(m, src, scalar=None, biased=False):
                if biased:
                    ins = V.tensor_tensor(x[:, m, :], x[:, m, :], src, ALU.add)
                elif scalar is None:
                    ins = V.scalar_tensor_tensor(x[:, m, :], x[:, m, :], ALPHA, src, ALU.mult, ALU.add)
                else:
                    ins = V.scalar_tensor_tensor(x[:, m, :], src, scalar, x[:, m, :], ALU.mult, ALU.add)
                ins.then_inc(S("res_ready"), 1)

            def square_residual(jobs0, mod=None, biased=False):
                for m in range(KT):
                    dve.wait_ge(S("square_done"), jobs0 + m // 2 + 1)
                    residual(m, pg[(m // 2) % 2][:, (m % 2) * T:(m % 2 + 1) * T],
                             None if mod is None else modv[:, mod + m, 0:1], biased)

            def down_residual(done0, mod=None):
                for m in range(KT):
                    dve.wait_ge(S("down_done"), done0 + m // 2 + 1)
                    residual(m, pd[:, m // 2, (m % 2) * T:(m % 2 + 1) * T],
                             None if mod is None else modv[:, mod + m, 0:1])

            def scaled(n, dst, gains, final=False):
                def low(k):
                    dve.wait_ge(S("x_high"), 8 * (n - 1) + k + 1)
                    V.tensor_tensor(xs[:, 1, k, :], dst[:, k, :], xs[:, 0, k, :].bitcast(F32), ALU.subtract
                                    ).then_inc(S("x_ready"), 1)

                for k in range(KT):
                    V.scalar_tensor_tensor(sq1[:, k, :], x[:, k, :], gains(k), nrm[:, 1, 0:T], ALU.mult, ALU.mult
                                           ).then_inc(S("x_scaled"), 1)
                    if k > 1 and not final:
                        low(k - 2)
                if not final:
                    low(KT - 2)
                    low(KT - 1)

            square_residual(0, 16)
            dve.wait_ge(S("res_ready"), 8)
            root(1, T, EPS_RMS)
            split_to(split0 + NSPLIT - 1)
            scaled(1, h1, lambda k: gain[:, k, 2:3])

            R = route
            lg = R[:, 0:40].rearrange("p (s c) -> p s c", s=2)
            gd, oh, gm = R[:, 40:48], R[:, 48:56], R[:, 56:58]
            gd3, oh3 = (v.rearrange("p (s c) -> p s c", s=2) for v in (gd, oh))
            seen, free = R[:, 58:60].unsqueeze(2), R[:, 60:62].unsqueeze(2)
            ein, o1, o2, etmp = (R[:, 62 + 8 * i:70 + 8 * i].rearrange("p (s c) -> p s c", s=2) for i in range(4))
            m1, m2 = R[:, 94:96], R[:, 96:98]
            ptop, pdiff, w1, w2 = R[:, 98:100], R[:, 100:102], R[:, 102:104], R[:, 104:106]
            e2 = R[:, 106:114].rearrange("p (s c) -> p s c", s=2)
            cmb = combine.rearrange("p (s g c) -> p s g c", s=2, g=4)

            def wide(v):
                return v.unsqueeze(2).to_broadcast([P, 2, 4])

            def first_hot(dst, values, top):
                then(V.tensor_tensor(dst, values, wide(top), ALU.is_equal))
                then(V.tensor_copy(seen, dst[:, :, 0:1]))
                for j in range(1, 4):
                    then(V.tensor_scalar(free, seen, -1.0, 1.0, ALU.mult, ALU.add))
                    then(V.tensor_tensor(seen, seen, dst[:, :, j:j + 1], ALU.max))
                    then(V.tensor_tensor(dst[:, :, j:j + 1], dst[:, :, j:j + 1], free, ALU.mult))

            dve.wait_ge(S("logits"), 1)
            then(V.tensor_copy(R[:, 0:40], pm[0][:, 0:40]))
            then(V.tensor_reduce(gm, lg[:, :, 0:4], AX, ALU.max))
            V.tensor_tensor(gd3, lg[:, :, 0:4], wide(gm), ALU.subtract).then_inc(S("group_diff"), 1)
            first_hot(oh3, lg[:, :, 0:4], gm)
            for g in range(4):
                dst = ein if g == 0 else etmp
                then(V.tensor_tensor(dst, lg[:, :, 4 + 4 * g:8 + 4 * g], oh3[:, :, g:g + 1].to_broadcast([P, 2, 4]),
                                     ALU.mult))
                if g:
                    then(V.tensor_tensor(ein, ein, etmp, ALU.add))
            then(V.tensor_reduce(m1, ein, AX, ALU.max))
            first_hot(o1, ein, m1)
            then(V.scalar_tensor_tensor(e2, o1, NEG, ein, ALU.mult, ALU.add))
            then(V.tensor_reduce(m2, e2, AX, ALU.max))
            first_hot(o2, e2, m2)
            V.tensor_tensor(pdiff, m2, m1, ALU.subtract).then_inc(S("pair_diff"), 1)
            dve.wait_ge(S("group_exp"), 1)
            then(V.tensor_reduce(gm, gd3, AX, ALU.add))
            then(V.reciprocal(ptop, gm))
            dve.wait_ge(S("pair_exp"), 1)
            then(V.tensor_scalar(m1, pdiff, 1.0, None, ALU.add))
            then(V.reciprocal(w1, m1))
            then(V.tensor_tensor(w1, w1, ptop, ALU.mult))
            then(V.tensor_tensor(w2, w1, pdiff, ALU.mult))
            then(V.tensor_tensor(o1, o1, wide(w1), ALU.mult))
            then(V.tensor_tensor(o2, o2, wide(w2), ALU.mult))
            then(V.tensor_tensor(o1, o1, o2, ALU.add))
            for g in range(4):
                last = V.tensor_tensor(cmb[:, :, g, :], o1, oh3[:, :, g:g + 1].to_broadcast([P, 2, 4]), ALU.mult)
            last.then_inc(S("combine"), 1)

            def ffn_hidden(u, s0, first, final, expert=None):
                e = s0 + (0 if first else 6 * (u - UFIRST[u]) - 2)
                for m in range(2):
                    split_to(e + 2 * m + 3)
                    up = pg[m][:, T:2 * T]
                    dve.wait_ge(S("silu_done"), 2 * u + m + 1)
                    if expert is not None:
                        then(V.tensor_tensor(utmp[:, m, :], up, comb[:, expert, :], ALU.mult))
                        up = utmp[:, m, :]
                    if u:
                        dve.wait_ge(S("hid_ready"), 2 * (u - 1) + m + 1)
                    V.tensor_tensor(htmp[:, m, :], silu_g[:, m, :], up, ALU.mult).then_inc(S("hid_raw"), 1)
                    dve.wait_ge(S("hid_high"), 2 * u + m + 1)
                    V.tensor_tensor(hid[:, u % 2, 1, m, :], htmp[:, m, :], hid[:, u % 2, 0, m, :].bitcast(F32),
                                    ALU.subtract).then_inc(S("hid_ready"), 1)
                if final:
                    split_to(s0 + 6 * (u - UFIRST[u] + 1) + 1)

            split_to(split0 + 3)
            dve.wait_ge(S("comb_out"), 8)
            for e in range(EXPERTS):
                ffn_hidden(e, split0, e == 0, e == EXPERTS - 1, e)
            down_residual(0, 40)
            dve.wait_ge(S("res_ready"), 16)
            root(2, T, EPS_RMS)
            scaled(2, x, lambda k: vec("norm_f_w", k))

            def attn_rotate(q):
                kind = KINDS[q // 4]
                start = QUNIT[q]

                def rope(e):
                    i = e % 2
                    nm = 1 if kind == 0 and i == 0 else 2
                    dve.wait_ge(S("rot_done"), e + 1)
                    cos, sin = (ropes[:, j, :].unsqueeze(1).to_broadcast([P, nm, T]) for j in range(2))
                    if e:
                        dve.wait_ge(S("rope_done"), e)
                    V.tensor_tensor(rt[:, 0, 0:nm, :], raw[:, i, 0:nm, :], cos, ALU.mult)
                    then(V.tensor_tensor(rt[:, 1, 0:nm, :],
                                         pm[0][:, 0:nm * T].rearrange("p (m t) -> p m t", t=T), sin, ALU.mult))
                    dst = (kr, qr)[i][:, e // 2 - PROJ[q], 0:nm, :]
                    V.tensor_tensor(dst, rt[:, 0, 0:nm, :], rt[:, 1, 0:nm, :], ALU.add).then_inc(S("rope_done"), 1)

                for g in range(GROUPS[kind]):
                    e = 2 * (PROJ[q] + g)
                    if g:
                        split_to(start + 3)
                        rope(e - 1)
                    end = start + (5 if kind else 4 if q % 4 == 0 else 2)
                    split_to(end + 2)
                    rope(e)
                    split_to(end + 3)
                    start = end + 1
                rope(2 * PROJ[q + 1] - 1)

            def attn_mask(q):
                layer, kind = q // 4, KINDS[q // 4]
                G = GROUPS[kind]
                for h in range(4):
                    for g in range(G):
                        u = 4 * PROJ[q] + h * G + g
                        dve.wait_ge(S("scored"), u + 1)
                        mask = masks[:, MASK_OF[kind][g], :]
                        V.scalar_tensor_tensor(s0[:, h, g * P:(g + 1) * P], pd[:, u % 2, 0:P], HD ** -0.5,
                                               mask[:, 0:P], ALU.mult, ALU.add)
                        last = V.scalar_tensor_tensor(s1[:, h, g * T:(g + 1) * T], pd[:, u % 2, P:P + T], HD ** -0.5,
                                                      mask[:, P:P + T], ALU.mult, ALU.add)
                        last.then_inc(S("masked"), 1)
                    if kind == 0:
                        sink = sinks[:, 16 * (layer // 3) + 4 * (q % 4) + h:16 * (layer // 3) + 4 * (q % 4) + h + 1]
                        V.tensor_copy(s0[:, h, P:P + 1], sink)
                        then(V.tensor_copy(s1[:, h, T:T + 1], sink))
                    else:
                        dve.wait_ge(S("masked"), 4 * PROJ[q] + (h + 1) * G)
                    ext = 1 if kind == 0 else 0
                    V.tensor_reduce(smx[:, 0, 0, h:h + 1], s0[:, h, 0:G * P + ext], AX, ALU.max, negate=True)
                    V.tensor_reduce(smx[:, 0, 1, h:h + 1], s1[:, h, 0:G * T + ext], AX, ALU.max, negate=True
                                    ).then_inc(S("smax"), 1)

            def attn_finish(q):
                dve.wait_ge(S("exped"), 4 * q + 4)
                then(V.reciprocal(smx[:, 2, :, :], smx[:, 1, :, :]))
                dve.wait_ge(S("o_done"), q + 1)
                for t in range(2):
                    last = V.tensor_tensor(osb[:, t, :, :], pg[t][:, 0:4 * HD].rearrange("p (h d) -> p h d", d=HD),
                                           smx[:, 2, t, :].unsqueeze(2).to_broadcast([P, 4, HD]), ALU.mult)
                last.then_inc(S("o_out"), 1)
                dve.wait_ge(S("oth_out"), q + 1)
                k = 2 * (q % 4)
                V.tensor_tensor(otl[:, k:k + 2, :], pd[:, 2, :].rearrange("p (k t) -> p k t", t=T),
                                oth[:, k:k + 2, :].bitcast(F32), ALU.subtract).then_inc(S("otl_out"), 1)

            def layer_norm(n):
                l = n - 3
                dve.wait_ge(S("ln_mean"), l + 1)
                for i in range(4):
                    sl = slice(2 * i, 2 * i + 2)
                    V.tensor_tensor(x[:, sl, :], x[:, sl, :],
                                    pm[0][:, 0:T].unsqueeze(1).to_broadcast([P, 2, T]), ALU.subtract
                                    ).then_inc(S("ln_centered"), 1)
                root(n, T, EPS_LN)
                o = 8 * (n - 3)
                scaled(n, x, lambda k: vec("ln_g", o + k), n == 2 + 2 * LAYERS)

            dve.wait_ge(S("masks_landed"), 16)
            for layer in range(LAYERS):
                q0 = 4 * layer
                attn_rotate(q0)
                for q in range(q0, q0 + 4):
                    attn_mask(q)
                    if q < q0 + 3:
                        attn_rotate(q + 1)
                    attn_finish(q)
                biased = KINDS[layer] == 0
                if biased:
                    dve.wait_ge(S("x_biased"), layer // 3 + 1)
                last = first[("wo", layer)] + 7
                for m in range(KT):
                    split_to(last - 7 + 2 * (m // 2) + 1 + 2)
                    dve.wait_ge(S("square_done"), 4 * (1 + layer) + m // 2 + 1)
                    residual(m, pg[(m // 2) % 2][:, (m % 2) * T:(m % 2 + 1) * T], None, biased)
                layer_norm(3 + 2 * layer)
                for j in range(NFF):
                    ffn_hidden(EXPERTS + NFF * layer + j, last + 1, j == 0, j == NFF - 1)
                down_residual(4 * (1 + layer))
                layer_norm(4 + 2 * layer)


PROJ = [0]
for _layer in range(LAYERS):
    for _quad in range(4):
        PROJ.append(PROJ[-1] + GROUPS[KINDS[_layer]])
VJOBS, QUNIT = [0], []
for _layer in range(LAYERS):
    for _quad in range(4):
        VJOBS.append(VJOBS[-1] + (GROUPS[KINDS[_layer]] if KINDS[_layer] else int(_quad == 0)))
        _key = [i for i, u in enumerate(plan()) if u[0:3] == ("qkv", _layer, _quad)]
        QUNIT.append(_key[0])
UFIRST = [0] * EXPERTS + [EXPERTS + NFF * layer for layer in range(LAYERS) for _ in range(NFF)]
NLOADS = 13
MAGIC = 12582912.0
PI32 = 3.1415925
TWO_PI_PARTS = (6.28125, 0.0019350051879882812, float(np.float32(TWO_PI - 6.28125 - 0.0019350051879882812)))
SEMAPHORES = ["loaded", "constants"]


def constants():
    c = np.zeros((P, NCONST), np.float32)
    p = np.arange(P)

    def put(name, v):
        v = np.asarray(v, np.float32).reshape(P, -1)
        c[:, COFF[name]:COFF[name] + v.shape[1]] = v

    put("ident", np.eye(P))
    put("flip", np.eye(P)[::-1])
    rot = np.zeros((P, P))
    for head in (0, HD):
        for d in range(8):
            rot[head + d + 8, head + d] = -1.0
            rot[head + d, head + d + 8] = 1.0
    put("rot", rot)
    ch = 2 * np.pi * np.outer(p, p) / P
    put("fn_c", np.concatenate([np.cos(ch), -np.sin(ch)], 1) / np.sqrt(float(T * P)))
    inv = np.float32(500000.0) ** (-np.arange(0, 16, 2, dtype=np.float32) / np.float32(16))
    d = p % HD
    put("freq", np.where(d < 16, inv[d % 8], 0.0))
    put("tcol", np.stack([-(p + s * P) / T for s in range(TT)], 1))
    put("drop0", np.stack([np.where(p == 0, NEG, 0.0), np.zeros(P)], 1))

    tok = np.arange(T)
    f = np.arange(T)
    ang = 2 * np.pi * np.outer(tok, f) / (2 * T)
    cos, nsin = np.cos(ang), -np.sin(ang)
    alt = (-1.0) ** tok
    sin_alt, cos_alt = nsin[:, :P].copy(), cos[:, :P].copy()
    sin_alt[:, 0] = alt
    cos_alt[:, 0] = alt
    fwd = np.concatenate([cos, sin_alt, nsin[:, P:], nsin[:, :P], cos_alt], 1)
    wgt = np.where(f == 0, 1.0, 2.0)[:, None] / (2 * T)
    back_im = 2.0 * nsin.T / (2 * T)
    back_im[0] = alt / (2 * T)
    back = np.concatenate([wgt * cos.T, back_im], 0)
    dft = np.concatenate([fwd.reshape(TT, P, 768).transpose(1, 0, 2).reshape(P, -1),
                          back.reshape(4, P, T).transpose(1, 0, 2).reshape(P, -1)], 1)

    lang = 2 * np.pi * np.outer(tok, tok) / T
    fn_l = np.stack([np.cos(lang), np.sin(lang)], 0).reshape(2, TT, P, T).transpose(2, 0, 1, 3).reshape(P, -1)
    key, query = tok[:, None], tok[None, :]
    ml = np.stack([np.where(key <= query, 0.0, NEG), np.where(key >= query, 0.0, NEG)], 0)
    ml = ml.reshape(2, TT, P, T).transpose(2, 0, 1, 3).reshape(P, -1)

    diff = tok[:, None] - tok[None, :]
    allowed = [(diff >= 0) & (diff <= 127), (diff >= 0) & (diff <= 128), (diff >= 0) & (diff % 4 == 0),
               (diff >= 0) & (diff % 16 == 0), diff >= 0]
    masks = np.stack([np.concatenate([m[:P, :P], m[P:, :]], 1) for m in (np.where(v, 0.0, NEG) for v in allowed)], 1)

    t = tok.astype(np.float32) / np.float32(T)
    bands = np.linspace(1e-4, 15, 16, dtype=np.float32)
    fang = np.float32(2 * np.pi) * t[:, None] * bands[None, :]
    feat = np.concatenate([t[:, None], np.cos(fang), np.sin(fang)], 1).T
    f32 = lambda v: np.ascontiguousarray(v, np.float32)
    return dict(consts=c, dft_tables=f32(dft), cx_tables=f32(np.concatenate([fn_l, ml], 1)),
                masks=f32(masks.reshape(P, -1)), feat=f32(feat))


def lay_out(v):
    def fm(u):
        return np.ascontiguousarray(u).reshape(-1, P).T

    def blocks(w):
        k, n = w.shape
        return w.reshape(k // P, P, n // P, P).transpose(1, 2, 0, 3).reshape(P, -1)

    def ktiles(w):
        return w.reshape(w.shape[0] // P, P, -1).transpose(1, 0, 2).reshape(P, -1)

    w_in, b_in = v["w_in"][0], v["b_in"][0]
    q0 = 4 * DB
    mlg, gate = q0 + 4 * DB, q0 + 4 * DB + 16
    parts = [(q0 + DB, DB), (q0, DB), (0, 3 * DB), (3 * DB, DB), (q0 + 3 * DB, DB), (gate, 3 * D)]
    cols = np.concatenate([np.arange(lo, lo + n) for lo, n in parts])
    taps = lambda w: w[0].reshape(9, -1, P).transpose(2, 1, 0).reshape(P, -1)
    vecs = dict(
        c=np.concatenate([fm(v["c"][0]), fm(v["c_ctx"])], 1), ada_b=fm(v["ada_b"][0]), norm1_w=fm(v["norm1_w"][0]),
        norm2_w=fm(v["norm2_w"][0]), norm_f_w=fm(v["norm_f_w"]), b_in=fm(b_in[cols]),
        hy_conv_w=taps(v["hy_conv_w"]), hy_conv_b=fm(v["hy_conv_b"][0]), ml_conv_w=taps(v["ml_conv_w"]),
        ml_conv_b=fm(v["ml_conv_b"][0]), hy_skip=fm(v["hy_skip"][0]), ml_norm_w=fm(v["ml_norm_w"][0]),
        ln_g=fm(v["ln_g_2"]), ln_b=fm(v["ln_b_2"]), a_bq=fm(v["a_b_qkv_2"][:, 0:D]),
        a_bk=fm(np.repeat(v["a_b_qkv_2"][:, D:D + T].reshape(2, 4, 1, HD), 2, axis=2)),
        a_bo=fm(v["a_b_o_2"]))
    rows = dict(b_v=b_in[q0 + 2 * DB:q0 + 3 * DB], b_gates=b_in[mlg:mlg + 16],
                b_route=np.concatenate([v["moe_rg_b"][0], v["moe_re_b"][0]]),
                a_bv=v["a_b_qkv_2"][:, D + T:].reshape(-1))
    a = dict(x=v["x"][0].T, ctx=v["ctx"][0].T,
             vecs=np.concatenate([vecs[n] for n, _ in VECS], 1),
             rows=np.concatenate([rows[n] for n, _ in ROWS])[None, :],
             hyf=np.stack([v["hy_f_b1"][0], v["hy_f_b2"][0], v["hy_f_freq"][0]], 1),
             hy_w1=v["hy_f_w1"][0], hy_w2=v["hy_f_w2"][0], hy_w3=v["hy_f_w3"][0],
             hy_decay=v["hy_decay"][0].reshape(-1), sinks=v["a_sinks_2"].reshape(-1),
             positions=v["positions_2"].reshape(-1),
             w_gates=ktiles(w_in[:, mlg:mlg + 16]).reshape(P, KT, 16),
             w_route=ktiles(np.concatenate([v["moe_rg_w"][0], v["moe_re_w"][0]], 1)).reshape(P, KT, 20))

    def columns(w, lo, n=P):
        return ktiles(w[:, lo:lo + n])

    win = np.concatenate([np.arange(q0 + 2 * DB, q0 + 3 * DB), cols])
    branch = np.stack([blocks(v["w_branch"][0, b]).reshape(P, KT, -1) for b in range(3)], 2).reshape(P, -1)

    def swiglu(gate, up, down, part):
        i = int(part[-1])
        if part.startswith("down"):
            return down[i * P:(i + 1) * P]
        return columns(gate if part.startswith("gate") else up, i * P)

    pieces = []
    for u in plan():
        if u[0] == "ada":
            piece = columns(v["ada_w"][0], u[1] * P)
        elif u[0] == "in":
            piece = ktiles(w_in[:, win[u[1] * P:(u[1] + 1) * P]])
        elif u[0] == "branch":
            piece = branch[:, u[1] * UNIT:(u[1] + 1) * UNIT]
        elif u[0] == "out":
            piece = columns(v["w_out"][0], u[1] * P)
        elif u[0] == "expert":
            piece = swiglu(v["moe_w_gate"][0, u[1]], v["moe_w_up"][0, u[1]], v["moe_w_down"][0, u[1]], u[2])
        elif isinstance(u[0], tuple):
            gu, lo = v["w_gate_up_2"][u[0][1]], u[1] * T
            piece = swiglu(gu[:, lo:lo + T], gu[:, FF + lo:FF + lo + T], v["w_down_2"][u[0][1]][lo:lo + T], u[2])
        elif u[0] == "wo":
            w = (v["a_w_o_2"][u[1] // 3], v["b_w_o_2"][0], v["c_w_o_2"][0])[KINDS[u[1]]]
            piece = columns(w, u[2] * P)
        else:
            _, layer, quad, part, i = u
            if KINDS[layer] == 0:
                w = v["a_w_qkv_2"][layer // 3]
                if part == "k":
                    wk = w[:, D + quad * HD:D + (quad + 1) * HD]
                    piece = ktiles(np.concatenate([wk, wk], 1))
                else:
                    piece = columns(w, (quad * T if part == "q" else D + T) + i * P)
            else:
                w = v["b_w_qkv_2"][0] if KINDS[layer] == 1 else v["c_w_qkv_2"][0]
                piece = columns(w, (3 * (i // 2) + "qkv".index(part)) * D + quad * T + (i % 2) * P)
        assert piece.shape == (P, UNIT), (u, piece.shape)
        pieces.append(piece)
    pieces = [np.concatenate(pieces[n:n + CHUNK], 1).reshape(-1) for n in range(0, len(pieces), CHUNK)]
    a["wstream"] = np.concatenate(pieces)
    return {k: np.ascontiguousarray(u) for k, u in a.items()}


def kernel(**inputs):
    import concourse.bacc as bacc
    from concourse.bass_utils import run_bass_kernel_spmd

    v = {k: np.asarray(u) for k, u in inputs.items()}
    arrays = {f"in_{k}": u for k, u in {**lay_out(v), **constants()}.items()}
    nc = bacc.Bacc("TRN2", target_bir_lowering=False, num_devices=1)
    aps = {k[3:]: nc.dram_tensor(k, u.shape, mybir.dt.from_np(u.dtype), kind="ExternalInput").ap()
           for k, u in arrays.items()}
    out = nc.dram_tensor("out_xt", (D, T), F32, kind="ExternalOutput").ap()
    build_program(nc, aps, out)
    r = run_bass_kernel_spmd(nc, [arrays], core_ids=[0])
    return np.ascontiguousarray(r.results[0]["out_xt"].T)[None]
```
